# Optimizing a Trainium2 kernel written in Bass

```python
import jax, jax.numpy as jnp
from jax import lax
import numpy as np

D_MODEL = 2048
BATCH = 1
SEQ = 256
DEPTH = 2

CHUNK = 64
Q_BLOCK = 128

MLA_HEADS = 8
MLA_Q_RANK = 512
MLA_KV_RANK = 512
MLA_NOPE = 128
MLA_ROPE = 64
MLA_V = 128
ROPE_THETA = 10000.0

GLA_HEADS = 4
GLA_DK = 128
GLA_DV = 256
GLA_GATE_RANK = 16
GLA_GATE_NORM = 16.0

SGU_BLOCK = 128
SGU_DFF = 2 * D_MODEL
SGU_HALF = SGU_DFF // 2
SGU_GROUPS = 16
SGU_GROUP_DIM = SGU_HALF // SGU_GROUPS

N_EXPERTS = 16
N_GROUPS = 4
EXPERTS_PER_GROUP = N_EXPERTS // N_GROUPS
GROUP_SCORE_K = 2
TOP_K = 2
D_EXPERT = 512

ALPHA = (2.0 * DEPTH) ** 0.25
BETA = (8.0 * DEPTH) ** -0.25
EPS = 1e-6

N_EVEN = (DEPTH + 1) // 2
N_ODD = DEPTH // 2

EVEN_WIDTHS = (MLA_Q_RANK, MLA_KV_RANK, MLA_ROPE,
               GLA_HEADS * GLA_DK, GLA_HEADS * GLA_DK, GLA_HEADS * GLA_DV,
               GLA_GATE_RANK, GLA_HEADS * GLA_DV)
EVEN_SPLITS = tuple(int(c) for c in np.cumsum(EVEN_WIDTHS)[:-1])
EVEN_IN = int(sum(EVEN_WIDTHS))
MIX_WIDTH = MLA_HEADS * MLA_V + GLA_HEADS * GLA_DV

kernel_name = "hybrid_mla_gla_gmlp_groupmoe_deepnorm"

def layer_norm(x, g, b):
    xf = x.astype(jnp.float32)
    mu = jnp.mean(xf, -1, keepdims=True)
    var = jnp.mean(jnp.square(xf - mu), -1, keepdims=True)
    return ((xf - mu) * lax.rsqrt(var + EPS) * g + b).astype(x.dtype)

def rms_norm(x, g):
    xf = x.astype(jnp.float32)
    return (xf * lax.rsqrt(jnp.mean(jnp.square(xf), -1, keepdims=True) + EPS) * g).astype(x.dtype)

def rope_tables(positions):
    inv = 1.0 / (ROPE_THETA ** (jnp.arange(0, MLA_ROPE, 2, dtype=jnp.float32) / MLA_ROPE))
    ang = positions.astype(jnp.float32)[..., None] * inv
    return jnp.cos(ang), jnp.sin(ang)

def apply_rope(x, cos, sin):
    x1, x2 = jnp.split(x.astype(jnp.float32), 2, axis=-1)
    return jnp.concatenate([x1 * cos - x2 * sin, x2 * cos + x1 * sin], -1).astype(x.dtype)

def mla(c_q, c_kv, k_rope, g_q, g_kv, w_uq, w_ukv, cos, sin):
    B, S, _ = c_q.shape
    q = jnp.einsum('bsr,rhd->bshd', rms_norm(c_q, g_q), w_uq)
    q_nope = q[..., :MLA_NOPE]
    q_rot = apply_rope(q[..., MLA_NOPE:], cos[:, :, None], sin[:, :, None])
    kv = jnp.einsum('bsr,rhd->bshd', rms_norm(c_kv, g_kv), w_ukv)
    k_nope, v = kv[..., :MLA_NOPE], kv[..., MLA_NOPE:]
    k_rot = apply_rope(k_rope, cos, sin)
    scale = (MLA_NOPE + MLA_ROPE) ** -0.5
    n_blk = S // Q_BLOCK
    qn = q_nope.reshape(B, n_blk, Q_BLOCK, MLA_HEADS, MLA_NOPE).transpose(1, 0, 2, 3, 4)
    qr = q_rot.reshape(B, n_blk, Q_BLOCK, MLA_HEADS, MLA_ROPE).transpose(1, 0, 2, 3, 4)
    key_chunk = jnp.arange(S) // CHUNK

    def block(args):
        i, qn_b, qr_b = args
        s = (jnp.einsum('bqhd,bkhd->bhqk', qn_b, k_nope)
             + jnp.einsum('bqhd,bkd->bhqk', qr_b, k_rot)).astype(jnp.float32) * scale
        q_chunk = (i * Q_BLOCK + jnp.arange(Q_BLOCK)) // CHUNK
        mask = key_chunk[None, :] <= q_chunk[:, None]
        p = jax.nn.softmax(jnp.where(mask, s, -jnp.inf), axis=-1).astype(v.dtype)
        return jnp.einsum('bhqk,bkhd->bqhd', p, v)

    o = lax.map(block, (jnp.arange(n_blk), qn, qr))
    return o.transpose(1, 0, 2, 3, 4).reshape(B, S, MLA_HEADS * MLA_V)

def gla(q, k, v, gate_lr, g_out, w_gk2, b_gk2, g_norm):
    B, S, _ = q.shape
    nc = S // CHUNK
    log_g = jax.nn.log_sigmoid((gate_lr @ w_gk2 + b_gk2).astype(jnp.float32)) / GLA_GATE_NORM
    qh = q.astype(jnp.float32).reshape(B, nc, CHUNK, GLA_HEADS, GLA_DK) * GLA_DK ** -0.5
    kh = k.astype(jnp.float32).reshape(B, nc, CHUNK, GLA_HEADS, GLA_DK)
    vh = v.astype(jnp.float32).reshape(B, nc, CHUNK, GLA_HEADS, GLA_DV)
    cum = jnp.cumsum(log_g.reshape(B, nc, CHUNK, GLA_HEADS, GLA_DK), axis=2)
    cum_end = cum[:, :, -1]
    k_dec = kh * jnp.exp(cum_end[:, :, None] - cum)
    upd = jnp.einsum('bclhk,bclhv->bchkv', k_dec, vh)
    decay = jnp.exp(cum_end)

    def step(state, inp):
        d, u = inp
        state = d[..., None] * state + u
        return state, state

    init = jnp.zeros((B, GLA_HEADS, GLA_DK, GLA_DV), jnp.float32)
    _, states = lax.scan(step, init, (decay.transpose(1, 0, 2, 3), upd.transpose(1, 0, 2, 3, 4)))
    o = jnp.einsum('bclhk,cbhkv->bclhv', qh, states)
    o = o.reshape(B, S, GLA_HEADS, GLA_DV).astype(q.dtype)
    o = rms_norm(o, g_norm) * jax.nn.silu(g_out.reshape(B, S, GLA_HEADS, GLA_DV))
    return o.reshape(B, S, GLA_HEADS * GLA_DV)

def spatial_gating(h, ln_g, ln_b, w_s, b_s):
    B, S, _ = h.shape
    u, v = h[..., :SGU_HALF], h[..., SGU_HALF:]
    v = layer_norm(v, ln_g, ln_b)
    nb = S // SGU_BLOCK
    vb = v.reshape(B, nb, SGU_BLOCK, SGU_GROUPS, SGU_GROUP_DIM)
    pos_chunk = jnp.arange(SGU_BLOCK) // CHUNK
    mask = pos_chunk[None, :] <= pos_chunk[:, None]
    w = jnp.where(mask[None], w_s, jnp.zeros_like(w_s))
    mixed = jnp.einsum('gij,bnjgc->bnigc', w, vb) + b_s.T[None, None, :, :, None]
    return u * mixed.reshape(B, S, SGU_HALF)

def grouped_moe(x, router_w, router_b, w_gate, w_up, w_down):
    B, S, D = x.shape
    t = x.reshape(B * S, D)
    scores = jax.nn.sigmoid((t @ router_w).astype(jnp.float32))
    biased = scores + router_b.astype(jnp.float32)
    grp = biased.reshape(-1, N_GROUPS, EXPERTS_PER_GROUP)
    grp_score = lax.top_k(grp, GROUP_SCORE_K)[0].sum(-1)
    best = jnp.argmax(grp_score, axis=-1)
    in_grp = jnp.repeat(jax.nn.one_hot(best, N_GROUPS, dtype=jnp.bool_), EXPERTS_PER_GROUP, axis=-1)
    _, idx = lax.top_k(jnp.where(in_grp, biased, -jnp.inf), TOP_K)
    gate = jnp.take_along_axis(scores, idx, axis=1)
    gate = gate / jnp.sum(gate, -1, keepdims=True)
    combine = jnp.einsum('tk,tke->te', gate, jax.nn.one_hot(idx, N_EXPERTS, dtype=jnp.float32)).astype(t.dtype)
    y = jnp.zeros_like(t)
    for e in range(N_EXPERTS):
        h = jax.nn.silu(t @ w_gate[e]) * (t @ w_up[e])
        y = y + combine[:, e:e + 1] * (h @ w_down[e])
    return y.reshape(B, S, D)

def setup_inputs(seed: int = 0) -> dict:
    key = jax.random.key(seed)
    ks = iter(jax.random.split(key, 32))
    nrm = lambda shape, s: jax.random.normal(next(ks), shape, jnp.float32) * s
    gain = lambda shape: 1.0 + nrm(shape, 0.02)
    offset = jax.random.randint(next(ks), (BATCH, 1), 0, 1024, jnp.int32) * CHUNK
    return {
        "x": nrm((BATCH, SEQ, D_MODEL), 1.0),
        "positions": offset + jnp.arange(SEQ, dtype=jnp.int32)[None, :],
        "ev_w_in": nrm((N_EVEN, D_MODEL, EVEN_IN), D_MODEL ** -0.5),
        "ev_q_norm": gain((N_EVEN, MLA_Q_RANK)),
        "ev_kv_norm": gain((N_EVEN, MLA_KV_RANK)),
        "ev_w_uq": nrm((N_EVEN, MLA_Q_RANK, MLA_HEADS, MLA_NOPE + MLA_ROPE), MLA_Q_RANK ** -0.5),
        "ev_w_ukv": nrm((N_EVEN, MLA_KV_RANK, MLA_HEADS, MLA_NOPE + MLA_V), MLA_KV_RANK ** -0.5),
        "ev_w_gk2": nrm((N_EVEN, GLA_GATE_RANK, GLA_HEADS * GLA_DK), GLA_GATE_RANK ** -0.5),
        "ev_b_gk2": nrm((N_EVEN, GLA_HEADS * GLA_DK), 0.1),
        "ev_gla_norm": gain((N_EVEN, GLA_DV)),
        "ev_w_out": nrm((N_EVEN, MIX_WIDTH, D_MODEL), MIX_WIDTH ** -0.5 * BETA),
        "od_w_in": nrm((N_ODD, D_MODEL, SGU_DFF), D_MODEL ** -0.5),
        "od_sgu_ln_g": gain((N_ODD, SGU_HALF)),
        "od_sgu_ln_b": nrm((N_ODD, SGU_HALF), 0.02),
        "od_w_s": nrm((N_ODD, SGU_GROUPS, SGU_BLOCK, SGU_BLOCK), SGU_BLOCK ** -0.5),
        "od_b_s": gain((N_ODD, SGU_GROUPS, SGU_BLOCK)),
        "od_w_out": nrm((N_ODD, SGU_HALF, D_MODEL), SGU_HALF ** -0.5 * BETA),
        "ln_mix_g": gain((DEPTH, D_MODEL)),
        "ln_mix_b": nrm((DEPTH, D_MODEL), 0.02),
        "ln_ffn_g": gain((DEPTH, D_MODEL)),
        "ln_ffn_b": nrm((DEPTH, D_MODEL), 0.02),
        "router_w": nrm((D_MODEL, N_EXPERTS), D_MODEL ** -0.5),
        "router_b": nrm((N_EXPERTS,), 0.01),
        "moe_w_gate": nrm((DEPTH, N_EXPERTS, D_MODEL, D_EXPERT), D_MODEL ** -0.5),
        "moe_w_up": nrm((DEPTH, N_EXPERTS, D_MODEL, D_EXPERT), D_MODEL ** -0.5),
        "moe_w_down": nrm((DEPTH, N_EXPERTS, D_EXPERT, D_MODEL), D_EXPERT ** -0.5 * BETA),
    }

def reference(x, positions, ev_w_in, ev_q_norm, ev_kv_norm, ev_w_uq, ev_w_ukv, ev_w_gk2,
              ev_b_gk2, ev_gla_norm, ev_w_out, od_w_in, od_sgu_ln_g, od_sgu_ln_b, od_w_s,
              od_b_s, od_w_out, ln_mix_g, ln_mix_b, ln_ffn_g, ln_ffn_b, router_w, router_b,
              moe_w_gate, moe_w_up, moe_w_down):
    cos, sin = rope_tables(positions)
    for i in range(DEPTH):
        j = i // 2
        if i % 2 == 0:
            h = x @ ev_w_in[j]
            c_q, c_kv, k_r, g_q, g_k, g_v, g_lr, g_o = jnp.split(h, EVEN_SPLITS, axis=-1)
            o_a = mla(c_q, c_kv, k_r, ev_q_norm[j], ev_kv_norm[j], ev_w_uq[j], ev_w_ukv[j], cos, sin)
            o_b = gla(g_q, g_k, g_v, g_lr, g_o, ev_w_gk2[j], ev_b_gk2[j], ev_gla_norm[j])
            mix = jnp.concatenate([o_a, o_b], axis=-1) @ ev_w_out[j]
        else:
            h = jax.nn.gelu(x @ od_w_in[j])
            mix = spatial_gating(h, od_sgu_ln_g[j], od_sgu_ln_b[j], od_w_s[j], od_b_s[j]) @ od_w_out[j]
        x = layer_norm(ALPHA * x + mix, ln_mix_g[i], ln_mix_b[i])
        ffn = grouped_moe(x, router_w, router_b, moe_w_gate[i], moe_w_up[i], moe_w_down[i])
        x = layer_norm(ALPHA * x + ffn, ln_ffn_g[i], ln_ffn_b[i])
    return x


_drawn_inputs = setup_inputs


def setup_inputs(seed=0):
    import zlib

    import numpy as np

    out = dict(_drawn_inputs(seed))
    spreads = {}
    factors = {'ev_q_norm': 8.0,
     'ev_kv_norm': 8.0,
     'ev_gla_norm': 8.0,
     'od_sgu_ln_g': 8.0,
     'od_sgu_ln_b': 16.099,
     'od_b_s': 18.724}
    for name, (base, spread) in spreads.items():
        noise = np.random.default_rng([zlib.crc32(name.encode()), seed]).standard_normal(out[name].shape)
        drawn = base * np.exp(spread * noise) if base else spread * noise
        out[name] = __import__('jax').numpy.asarray(drawn.astype(out[name].dtype))
    for name, factor in factors.items():
        out[name] = (out[name] * factor).astype(out[name].dtype)
    return out
```

```python
from contextlib import ExitStack

import numpy as np

import concourse.bass as bass
from concourse import mybir

ALU = mybir.AluOpType
ACT = mybir.ActivationFunctionType
AX_X = mybir.AxisListType.X
F32 = mybir.dt.float32
F32R = mybir.dt.float32r
I32 = mybir.dt.int32

P = 128
D = 2048
SEQ = 256
TT = SEQ // P
KT = D // P
NB = 512
NBLK = D // NB
DEPTH = 2
CHUNK = 64
HEADS, NOPE, ROPE, VD = 8, 128, 64, 128
HALF = ROPE // 2
RANK = 512
GH, GDK, GDV, GRANK = 4, 128, 256, 16
W_IN = 4176
CQ, CKV, KR, GQ, GK, GV, LR, GO = 0, 512, 1024, 1088, 1600, 2112, 3136, 3152
GROUPS = 16
NEXP, NGRP, EPG, DEXP = 16, 4, 4, 512
NPAIR = NEXP // 2
CAP = 128
ALPHA = (2.0 * DEPTH) ** 0.25
EPS = 1e-6
BIG = 3.0e38
FAR = 4096.0
C2PI_A, C2PI_B = 6.28125, 0.0019350051879882812
C2PI_C = 2 * np.pi - C2PI_A - C2PI_B
PI_IN = 3.1415925
ROUND = 12582912.0

IN0_FULL = 8
SB_IN0, SB_OUT0 = 0, 9
SB_MOE0 = SB_OUT0 + NBLK
SB_IN1 = SB_MOE0 + 3 * NEXP
SB_OUT1 = SB_IN1 + 8
SB_MOE1 = SB_OUT1 + NBLK
N_ATT_BLOCKS = 2
PAIR_BLOCKS = ((0, 0), (0, 1), (1, 0), (0, 2), (1, 1), (1, 2))
POOL_SLOTS = (0, 2)
T_IN0, T_OUT0, T_R0, T_IN1, T_OUT1, T_R1 = range(0, 48, 8)


def land_block(sb):
    return sb + (N_ATT_BLOCKS if sb >= SB_OUT0 else 0)


CONST = {}
_at = 0
for _n, _w in [("ident", P), ("lower", P), ("ones", P), ("suffix", P), ("chunk_of", 2), ("iota0", P), ("iota1", P),
               ("inv_freq", HALF), ("four", NGRP), ("sixteen", NEXP)]:
    CONST[_n] = (_at, _at + _w)
    _at += _w
CW = _at


def constants():
    c = np.zeros((P, CW), np.float32)
    i = np.arange(P)

    def put(name, value):
        a, b = CONST[name]
        c[:, a:b] = value

    put("ident", np.eye(P))
    put("lower", i[:, None] < i[None, :])
    put("ones", 1.0)
    same = (i[:, None] // CHUNK) == (i[None, :] // CHUNK)
    put("suffix", ((i[:, None] > i[None, :]) & same) / 16.0)
    put("chunk_of", ((i[:, None] // CHUNK) == np.arange(2)[None, :]) / 16.0)
    put("iota0", i[None, :])
    put("iota1", CAP + i[None, :])
    put("inv_freq", (np.float32(1) / (10000.0 ** (np.arange(0, ROPE, 2) / ROPE)).astype(np.float32))[None, :])
    put("four", (NGRP - np.arange(NGRP))[None, :])
    put("sixteen", (NEXP - np.arange(NEXP))[None, :])
    return c


FILLS = (
    [("gqT", t, "a") for t in range(TT)] + [("lrT", 0, "a")]
    + [("cqT", t, "v") for t in range(TT)] + [("ckvT", t, "v") for t in range(TT)]
    + [("krT", 0, "a")]
    + [("z", t, "v") for t in range(TT)]
    + [("qr", t, "v") for t in range(TT)]
    + [("qn", i, "a") for i in range(4)]
    + [("suf", t, "a") for t in range(TT)] + [("dec", 0, "a")]
    + [("upd", i, "v") for i in range(8)]
    + [("kn", i, "a") for i in range(4)] + [("v", i, "a") for i in range(4)]
    + [("qrT", i, "a") for i in range(4)]
    + [("ob", i, "v") for i in range(4)]
    + [("s", i, "a") for i in range(6)]
    + [("pT", i, "a") for i in range(6)]
    + [("o", i, "v") for i in range(4)]
)
FILL_AT = {(n, i): k for k, (n, i, _) in enumerate(FILLS)}
EMPTIED = {}
for _who in "av":
    for _k, (_n, _i, _w) in enumerate([f for f in FILLS if f[2] == _who]):
        EMPTIED[(_n, _i)] = (_who, _k + 1)


def build(nc, A, out):
    with ExitStack() as ctx:
        def sem(name):
            return ctx.enter_context(nc.semaphore(name))

        at = [0]

        def sb(name, shape, dt=F32, offset=None):
            size = 4 * int(np.prod(shape[1:]))
            if offset is None:
                offset = at[0]
                at[0] += (size + 31) // 32 * 32
            return nc.alloc_sbuf_tensor_at(name, shape, dt, offset=base + offset)

        base = (nc.sbuf_base + 63) // 64 * 64

        w_land = sb("w_land", [P, 4, 4 * NB])
        split_at = at[0]
        w_hi = sb("w_hi", [P, 4, 4 * NB], F32R)
        w_lo = sb("w_lo", [P, 4, 4 * NB], F32R)
        X = sb("X", [P, TT, D])
        t_at = at[0]
        T_hi = sb("T_hi", [P, KT * SEQ], F32R)
        T_lo = sb("T_lo", [P, KT * SEQ], F32R)
        rows_at = at[0]
        rows = sb("rows", [P, 2, D])
        const = sb("const", [P, CW])
        rw_hi = sb("rw_hi", [P, KT, NEXP], F32R)
        rw_lo = sb("rw_lo", [P, KT, NEXP], F32R)
        rbias = sb("rbias", [P, NEXP])
        gains = sb("gains", [P, 2, 4])
        gnorm = sb("gnorm", [P, GDV])
        small = sb("small", [P, 160])
        flag = sb("flag", [P, DEPTH], I32)
        flagf = sb("flagf", [P, DEPTH])
        b_at = at[0]

        xT_hi = T_hi[:, :].rearrange("p (t s) -> p t s", t=KT)
        xT_lo = T_lo[:, :].rearrange("p (t s) -> p t s", t=KT)
        x_hi = T_hi[:, :].rearrange("p (a d) -> p a d", a=TT)
        x_lo = T_lo[:, :].rearrange("p (a d) -> p a d", a=TT)

        def cst(name, n=P):
            a, b = CONST[name]
            return const[0:n, a:b]

        ident = cst("ident")

        H = sb("H", [P, TT, W_IN], offset=b_at)
        r_at = b_at + TT * W_IN * 4
        cosT = sb("cosT", [P, TT, HALF], offset=r_at)
        sinT = sb("sinT", [P, TT, HALF], offset=r_at + 256)
        ropet = sb("ropet", [P, 4, TT, HALF], offset=r_at + 512)
        posi = sb("posi", [P, TT], I32, offset=r_at + 1536)
        posf = sb("posf", [P, TT], offset=r_at + 1568)
        rw_land = sb("rw_land", [P, KT, NEXP], offset=r_at + 1600)
        kr_rot = sb("kr_rot", [P, TT, ROPE], offset=r_at + 2624)
        st_at = r_at + 3136
        att = sb("att", [P, 96], offset=st_at)
        o = [split_at]

        def over(name, shape, where=o):
            t = sb(name, shape, offset=where[0])
            where[0] += 4 * int(np.prod(shape[1:]))
            return t

        qnT = over("qnT", [P, HEADS, SEQ])
        knT = over("knT", [P, HEADS, SEQ])
        vv = over("vv", [P, TT, HEADS * VD])
        qrT = over("qrT", [ROPE, HEADS, SEQ])
        sc_at = o[0]
        S0 = over("S0", [P, HEADS, P])
        S1 = over("S1", [P, HEADS, SEQ])
        pT0 = over("pT0", [P, HEADS, P])
        pT1 = over("pT1", [P, HEADS, TT, P])
        states = sb("states", [P, GH, 4, GDV], offset=sc_at)
        qrr = over("qrr", [P, TT, HEADS, ROPE])
        assert o[0] <= t_at - 4 * TT * D
        o2 = [t_at]
        cqT = over("cqT", [P, 4, SEQ], o2)
        ckvT = over("ckvT", [P, 4, SEQ], o2)
        gqT = over("gqT", [P, GH, SEQ], o2)
        lg = over("lg", [P, TT, GH * GDK], o2)
        kdec = over("kdec", [P, TT, GH * GDK], o2)
        la = over("la", [P, TT, GH * GDK], o2)
        krT = over("krT", [ROPE, SEQ], o2)
        lrT = over("lrT", [32, SEQ], o2)
        dec = over("dec", [P, GH, 4], o2)
        rtmp = over("rtmp", [P, 2, HEADS, HALF], o2)
        assert o2[0] <= t_at + 2 * 4 * KT * SEQ
        o3 = [b_at]

        def moe_buf(name, shape, dt=F32):
            t = sb(name, shape, dt, offset=o3[0])
            o3[0] += (4 * int(np.prod(shape[1:])) + 31) // 32 * 32
            return t

        xg_hi = sb("xg_hi", [P, KT, 2 * CAP], F32R, offset=rows_at)
        xg_lo = moe_buf("xg_lo", [P, KT, 2 * CAP], F32R)
        hT_hi = moe_buf("hT_hi", [P, 4, CAP], F32R)
        hT_lo = moe_buf("hT_lo", [P, 4, CAP], F32R)
        hid = moe_buf("hid", [P, DEXP])
        gsil = moe_buf("gsil", [P, DEXP])
        y_hi = moe_buf("y_hi", [P, 2, NB], F32R)
        y_lo = moe_buf("y_lo", [P, 2, NB], F32R)
        place_r = moe_buf("place_r", [P, TT, 2 * CAP], F32R)
        place = moe_buf("place", [P, TT, CAP])
        placeT = moe_buf("placeT", [P, SEQ], F32R)
        route = moe_buf("route", [P, 16, TT, NEXP])
        rank = moe_buf("rank", [P, TT, NEXP])
        comb = moe_buf("comb", [P, TT, NEXP])
        cur = moe_buf("cur", [P, 4, TT])
        rt_hi = sb("rt_hi", [P, 2, 4, P], F32R, offset=b_at)
        rt_lo = sb("rt_lo", [P, 2, 4, P], F32R, offset=b_at + 4096)
        o4 = [b_at]
        UV = over("UV", [P, TT, 2 * D], o4)
        U, V = UV[:, :, 0:D], UV[:, :, D:2 * D]
        ws = over("ws", [P, GROUPS, P], o4)
        bs = over("bs", [GROUPS, P], o4)
        bsT = over("bsT", [P, GROUPS], o4)
        wsT = sb("wsT", [P, GROUPS, P], offset=t_at)
        end = max(st_at + 400, o3[0], o4[0])
        assert base + end <= nc.sbuf_usable_end, (base + end, nc.sbuf_usable_end)

        stats = small[:, 0:TT * 4 * 6].rearrange("p (a n s) -> p a n s", a=TT, n=4)
        meanvar = small[:, 48:52].rearrange("p (a s) -> p a s", a=TT)
        inv_var = small[:, 52:54]
        rstd = small[:, 54:56]
        shift = small[:, 56:58]

        bank = [ctx.enter_context(nc.psum_tensor(f"bank{i}", [P, NB], F32)) for i in range(8)]

        const_in, x_in, rows_in, ws_in = sem("const_in"), sem("x_in"), sem("rows_in"), sem("ws_in")
        out_stored = sem("out_stored")
        t_filled, t_high, t_low = sem("t_filled"), sem("t_high"), sem("t_low")
        gemm_out_a, gemm_out_v = sem("gemm_out_a"), sem("gemm_out_v")
        rows_used = sem("rows_used")
        ln_recip, ln_root, ln_shift, ln_scaled, x_ready = (sem(n) for n in ("ln_recip", "ln_root", "ln_shift",
                                                                              "ln_scaled", "x_ready"))
        rw_high, rw_split = sem("rw_high"), sem("rw_split")
        att_filled, att_out_a, att_out_v = sem("att_filled"), sem("att_out_a"), sem("att_out_v")
        bias_in = sem("bias_in")
        trig_ready, trig_done = sem("trig_ready"), sem("trig_done")
        rms_sq, rms_rec, rms_root, c_normed, kr_rotated, ones_set = (sem(n) for n in (
            "rms_sq", "rms_rec", "rms_root", "c_normed", "kr_rotated", "ones_set"))
        z_soft, logg_ready, kdec_ready, go_silu, ob_sq, ob_rec, ob_root = (sem(n) for n in (
            "z_soft", "logg_ready", "kdec_ready", "go_silu", "ob_sq", "ob_rec", "ob_root"))
        qr_rotated, s_shifted, p_ready = (sem(n) for n in ("qr_rotated", "s_shifted", "p_ready"))
        x_high, x_low = sem("x_high"), sem("x_low")
        logits_done, sigm_done, sel_ready, rank_done, rank_ready, flag_ready, x_scaled = (sem(n) for n in (
            "logits_done", "sigm_done", "sel_ready", "rank_done", "rank_ready", "flag_ready", "x_scaled"))
        sgu_filled, sgu_out, wsT_copied, wsT_ready, v_ready, moe_over = (sem(n) for n in (
            "sgu_filled", "sgu_out", "wsT_copied", "wsT_ready", "v_ready", "moe_over"))
        chain_a, chain_v = sem("chain_a"), sem("chain_v")

        class Stream:

            def __init__(self, tag):
                def s(name):
                    return sem(tag + name)

                self.landed = [s(f"landed{j}") for j in range(4)]
                self.lo_done = [s(f"lo_done{j}") for j in range(4)]
                self.hi_done, self.used = s("hi_done"), s("used")
                self.xg_fill_h, self.xg_fill_l = s("xg_fill_h"), s("xg_fill_l")
                self.xg_out_h, self.xg_out_l = s("xg_out_h"), s("xg_out_l")
                self.silu_done, self.h_done, self.hT_fill = s("silu_done"), s("h_done"), s("hT_fill")
                self.hT_hi_done, self.hT_lo_done = s("hT_hi_done"), s("hT_lo_done")
                self.cur_ready, self.cur_seen, self.cur_v = s("cur_ready"), s("cur_seen"), s("cur_v")
                self.place_ready, self.place_r_ready = s("place_ready"), s("place_r_ready")
                self.pt_fill, self.pt_done = s("pt_fill"), s("pt_done")
                self.y_hi_done, self.y_lo_done, self.scat_fill = s("y_hi_done"), s("y_lo_done"), s("scat_fill")
                self.acc0_done, self.acc_done = s("acc0_done"), s("acc_done")

        main = Stream("")
        overflow = [Stream(f"over{layer}_") for layer in range(DEPTH)]
        landed = main.landed

        def ge(eng, s, value):
            if not (isinstance(value, int) and value <= 0):
                eng.wait_ge(s, value)

        class Chain:

            def __init__(self, eng, s):
                self.eng, self.s, self.n = eng, s, 0

            def __call__(self, ins):
                self.n += 1
                ins.then_inc(self.s, 1)

            def wait(self):
                self.eng.wait_ge(self.s, self.n)

        w_in0 = A["ev_w_in"][0].rearrange("(p t) n -> p t n", t=KT)
        w_in1 = A["od_w_in"][0].rearrange("(p t) n -> p t n", t=KT)
        w_out1 = A["od_w_out"][0].rearrange("(p t) n -> p t n", t=KT)
        w_out0 = A["ev_w_out"][0].rearrange("(h p t) n -> h p t n", h=2, t=KT // 2)
        w_uq = A["ev_w_uq"][0].rearrange("(p c) h d -> p c h d", c=4)
        w_ukv = A["ev_w_ukv"][0].rearrange("(p c) h d -> p c h d", c=4)
        out_v = out.rearrange("b (a p) d -> p (b a) d", p=P)
        x_v = A["x"].rearrange("b (a p) d -> p (b a) d", p=P)
        pos_v = A["positions"].rearrange("b (a p) -> p (b a)", p=P)

        def land(j, n=NB):
            return w_land[:, j, 0:4 * n].rearrange("p (c n) -> p c n", c=4)

        def hi(j, n=NB):
            return w_hi[:, j, 0:4 * n].rearrange("p (c n) -> p c n", c=4)

        def lo(j, n=NB):
            return w_lo[:, j, 0:4 * n].rearrange("p (c n) -> p c n", c=4)

        def moe_src(layer, e, part, j):
            if part < 2:
                w = A[("moe_w_gate", "moe_w_up")[part]][layer, bass.ds(e, 1)]
                return w.rearrange("o (p t) n -> (o p) t n", t=KT)[:, 4 * j:4 * j + 4, :]
            w = A["moe_w_down"][layer, bass.ds(e, 1)]
            return w.rearrange("o (p t) n -> (o p) t n", t=4)[:, :, j * NB:(j + 1) * NB]

        def over_pairs(eng, body):
            body(0, True, False)
            with eng.Fori(1, NPAIR - 1) as p:
                body(p, False, False)
            body(NPAIR - 1, False, True)

        block = ctx.enter_context(nc.Block())

        @block.sync
        def _(sp):
            sp.dma_start(X[:, 0, :], x_v[:, 0, :]).then_inc(x_in, 16)
            sp.dma_start(X[:, 1, :], x_v[:, 1, :]).then_inc(x_in, 16)

            def load(lb, j, src, s=main, n=NB):
                sp.dma_start(land(j, n), src).then_inc(s.landed[j], 16)

            for j in range(4):
                load(0, j, w_in0[:, 4 * j:4 * j + 4, 0:NB])
            with sp.Fori(1, IN0_FULL) as b:
                for j in range(4):
                    sp.wait_ge(main.lo_done[j], b)
                    load(b, j, w_in0[:, 4 * j:4 * j + 4, bass.ds(b * NB, NB)])
            tail = W_IN - IN0_FULL * NB
            for j in range(4):
                sp.wait_ge(main.lo_done[j], IN0_FULL)
                load(IN0_FULL, j, w_in0[:, 4 * j:4 * j + 4, IN0_FULL * NB:W_IN], n=tail)
            att_units = (
                [None, w_uq[:, :, :, NOPE:NOPE + ROPE], w_uq[:, :, 0:4, 0:NOPE], w_uq[:, :, 4:8, 0:NOPE]],
                [w_ukv[:, :, 0:4, 0:NOPE], w_ukv[:, :, 4:8, 0:NOPE], w_ukv[:, :, 0:4, NOPE:], w_ukv[:, :, 4:8, NOPE:]],
            )
            for b in range(2):
                for j in range(4):
                    if b == 0:
                        sp.wait_ge(main.lo_done[j], IN0_FULL + 1)
                    else:
                        sp.wait_ge(att_filled, FILL_AT[(("z", 1), ("qr", 1), ("qn", 1), ("qn", 3))[j]] + 1)
                    if b == 0 and j == 0:
                        sp.dma_start(w_land[0:GRANK, 0, 0:NB], A["ev_w_gk2"][0]).then_inc(landed[0], 16)
                        sp.dma_start(w_land[GRANK:GRANK + 1, 0, 0:NB], A["ev_b_gk2"]).then_inc(bias_in, 16)
                        continue
                    src = att_units[b][j]
                    heads = src.shape[2]
                    sp.dma_start(w_land[:, j, :].rearrange("p (c h d) -> p c h d", c=4, h=heads), src) \
                        .then_inc(landed[j], 16)
            for b in range(NBLK):
                for j in range(4):
                    if b == 0:
                        sp.wait_ge(att_filled, FILL_AT[(("kn", 1), ("kn", 3), ("v", 1), ("v", 3))[j]] + 1)
                    else:
                        sp.wait_ge(main.lo_done[j], SB_OUT0 + b)
                    load(0, j, w_out0[j // 2, :, 4 * (j % 2):4 * (j % 2) + 4, b * NB:(b + 1) * NB])

            def experts(layer, s, sb0):
                def body(p, first, last):
                    for b, (k, part) in enumerate(PAIR_BLOCKS):
                        for j in range(4):
                            if not (first and b == 0 and sb0 == 0):
                                sp.wait_ge(s.lo_done[j], sb0 + 6 * p + b)
                            load(0, j, moe_src(layer, 2 * p + k, part, j), s)
                over_pairs(sp, body)

            def overflow_pass(layer):
                sp.wait_ge(flag_ready, layer + 1)
                many = sp.value_load(flag[0:1, layer:layer + 1])
                with sp.If(many > CAP):
                    for j in range(4):
                        sp.wait_ge(main.lo_done[j], (SB_MOE0, SB_MOE1)[layer] + 3 * NEXP)
                    experts(layer, overflow[layer], 0)
                    for j in range(4):
                        sp.wait_ge(overflow[layer].lo_done[j], 3 * NEXP)

            experts(0, main, SB_MOE0)
            overflow_pass(0)
            with sp.Fori(0, 8) as b:
                for j in range(4):
                    sp.wait_ge(main.lo_done[j], SB_IN1 + b)
                    load(0, j, w_in1[:, 4 * j:4 * j + 4, bass.ds(b * NB, NB)])
            for b in range(NBLK):
                for j in range(4):
                    sp.wait_ge(main.lo_done[j], SB_OUT1 + b)
                    load(0, j, w_out1[:, 4 * j:4 * j + 4, b * NB:(b + 1) * NB])
            experts(1, main, SB_MOE1)
            overflow_pass(1)
            for k in range(TT * NBLK):
                a, n = k // NBLK, k % NBLK
                sp.wait_ge(x_ready, 3 * TT * NBLK + k + 1)
                sp.dma_start(out_v[:, a, n * NB:(n + 1) * NB], X[:, a, n * NB:(n + 1) * NB]).then_inc(out_stored, 16)
            sp.wait_ge(out_stored, 16 * TT * NBLK)

        @block.gpsimd
        def _(pool):
            for dst, src in ((const[:], A["const"]), (rw_land[:], A["router_w"].rearrange("(p t) e -> p t e", t=KT)),
                             (rbias[:], A["router_b"].rearrange("(o e) -> o e", o=1).partition_broadcast(P)),
                             (gains[:, 0, :], A["ev_q_norm"][0].rearrange("(p t) -> p t", t=4)),
                             (gains[:, 1, :], A["ev_kv_norm"][0].rearrange("(p t) -> p t", t=4)),
                             (gnorm[:], A["ev_gla_norm"].partition_broadcast(P)),
                             (posi[:], pos_v)):
                pool.dma_start(dst, src, allow_slow_non_contiguous=True).then_inc(const_in, 16)

            def load_rows(g, b, n):
                if n:
                    pool.wait_ge(rows_used, n)
                pool.dma_start(rows[:, 0, :], g.partition_broadcast(P)).then_inc(rows_in, 16)
                pool.dma_start(rows[:, 1, :], b.partition_broadcast(P)).then_inc(rows_in, 16)

            def experts(layer, s, sb0, p0, iota):
                def one_hot(dst, k, col):
                    for a in range(TT):
                        ins = pool.tensor_scalar(dst[:, a, k * CAP:(k + 1) * CAP], cst(iota), cur[:, col, a:a + 1],
                                                 None, ALU.is_equal)
                    return ins

                def ranks_read(count):
                    pool.wait_ge(s.cur_ready, count)
                    pool.sem_inc(s.cur_seen, 1)

                def one(e, count):
                    pool.tensor_copy(cur[:, 0, :], rank[:, :, bass.ds(e, 1)].rearrange("p a o -> p (a o)")) \
                        .then_inc(s.cur_ready, 1)
                    ranks_read(count)
                    one_hot(place, 0, 0).then_inc(s.place_ready, 1)

                def pair(p, count):
                    pool.tensor_copy(cur[:, 1:3, :], rank[:, :, bass.ds(2 * p, 2)].rearrange("p a o -> p o a")) \
                        .then_inc(s.cur_ready, 1)
                    ranks_read(count)
                    one_hot(place_r, 0, 1)
                    one_hot(place_r, 1, 2).then_inc(s.place_r_ready, 1)

                def body(p, first, last):
                    C, E = 3 * (p0 + p) + 1, 2 * (p0 + p)
                    ge(pool, s.pt_fill, E)
                    one(2 * p, C + 1)
                    if not last:
                        pool.wait_ge(s.xg_fill_l, 8 * (p0 + p + 1))
                        pair(p + 1, C + 2)
                    pool.wait_ge(s.pt_fill, E + 1)
                    one(2 * p + 1, C + (2 if last else 3))
                    for b in (4,) if last else (4, 6):
                        for j in POOL_SLOTS:
                            pool.wait_ge(s.hi_done, 4 * (sb0 + 6 * p + b) + j + 1)
                            pool.tensor_tensor(w_lo[:, j, :], w_land[:, j, :], w_hi[:, j, :], ALU.subtract) \
                                .then_inc(s.lo_done[j], 1)

                pair(0, 3 * p0 + 1)
                if s is main:
                    pool.wait_ge(t_filled, (T_R0, T_R1)[layer] + 8)
                    for a in range(TT):
                        ins = pool.tensor_scalar(X[:, a, :], X[:, a, :], ALPHA, None, ALU.mult)
                    ins.then_inc(x_scaled, 1)
                over_pairs(pool, body)

            def moe(layer):
                pool.wait_ge(rank_ready, layer + 1)
                pool.wait_ge(flag_ready, layer + 1)
                experts(layer, main, (SB_MOE0, SB_MOE1)[layer], layer * NPAIR, "iota0")
                many = pool.value_load(flag[0:1, layer:layer + 1])
                with pool.If(many > CAP):
                    pool.wait_ge(main.scat_fill, 4 * NEXP * (layer + 1))
                    experts(layer, overflow[layer], 0, 0, "iota1")
                    pool.wait_ge(overflow[layer].h_done, NEXP)
                pool.wait_ge(main.h_done, NEXP * (layer + 1))
                load_rows(A["ln_ffn_g"][layer:layer + 1], A["ln_ffn_b"][layer:layer + 1], (1, 4)[layer])

            load_rows(A["ln_mix_g"][0:1], A["ln_mix_b"][0:1], 0)
            pool.wait_ge(const_in, 16 * 7)
            moe(0)
            load_rows(A["od_sgu_ln_g"], A["od_sgu_ln_b"], 2)
            pool.wait_ge(moe_over, 1)
            pool.dma_start(ws[:], A["od_w_s"][0].rearrange("g i j -> i g j")).then_inc(ws_in, 16)
            pool.dma_start(bs[:], A["od_b_s"][0]).then_inc(ws_in, 16)
            load_rows(A["ln_mix_g"][1:2], A["ln_mix_b"][1:2], 3)
            moe(1)

        @block.tensor
        def _(pe):
            def three(dst, hi_l, lo_l, hi_r, lo_r, start, stop):
                pe.matmul(dst, hi_l, hi_r, start=start, stop=False)
                pe.matmul(dst, hi_l, lo_r, start=False, stop=False)
                return pe.matmul(dst, lo_l, hi_r, start=False, stop=stop)

            def transposes(t0, src, ready):
                for g in range(8):
                    a, q = g // 4, g % 4
                    ready(a, q)
                    if g >= 2:
                        pe.wait_ge(t_low, t0 + g - 1)
                    for c in range(4):
                        ins = pe.transpose(bank[4 + g % 2][:, c * P:(c + 1) * P], src(a, 4 * q + c), ident)
                    ins.then_inc(t_filled, 1)

            def gemm_block(sb, pair, n=NB):
                for j in range(4):
                    pe.wait_ge(main.lo_done[j], sb + 1)
                    for a in range(TT):
                        for c in range(4):
                            t = 4 * j + c
                            ins = three(bank[2 * pair + a][:, 0:n], xT_hi[:, t, a * P:(a + 1) * P],
                                        xT_lo[:, t, a * P:(a + 1) * P], hi(j, n)[:, c, :], lo(j, n)[:, c, :],
                                        t == 0, t == KT - 1)
                    ins.then_inc(main.used, 1)

            pe.wait_ge(const_in, 16 * 7)
            pe.wait_ge(x_in, 32)
            transposes(T_IN0, lambda a, t: X[:, a, t:D:KT], lambda a, q: None)
            pe.wait_ge(t_low, T_IN0 + 8)
            gemm_block(0, 0)
            gemm_block(1, 1)
            with pe.Fori(1, IN0_FULL // 2) as i:
                for p in range(2):
                    pe.wait_ge(gemm_out_a, 2 * i + p - 1)
                    pe.wait_ge(gemm_out_v, 2 * i + p - 1)
                    gemm_block(2 * i + p, p)
            pe.wait_ge(gemm_out_a, IN0_FULL - 1)
            pe.wait_ge(gemm_out_v, IN0_FULL - 1)
            gemm_block(IN0_FULL, 0, W_IN - IN0_FULL * NB)
            pe.wait_ge(gemm_out_a, IN0_FULL + 1)
            pe.wait_ge(gemm_out_v, IN0_FULL + 1)

            def begin(name, i=0):
                k = FILL_AT[(name, i)]
                if k >= 8:
                    emptied(*FILLS[k - 8][:2])
                return bank[k % 8]

            def emptied(name, i=0):
                who, n = EMPTIED[(name, i)]
                pe.wait_ge(att_out_a if who == "a" else att_out_v, n)

            def end(ins):
                ins.then_inc(att_filled, 1)

            for a in range(TT):
                b = begin("gqT", a)
                for h in range(GH):
                    ins = pe.transpose(b[:, h * P:(h + 1) * P], H[:, a, GQ + h * GDK:GQ + (h + 1) * GDK], ident)
                end(ins)
            b = begin("lrT")
            for a in range(TT):
                ins = pe.transpose(b[0:GRANK, a * P:(a + 1) * P], H[:, a, LR:LR + GRANK], ident)
            end(ins)
            for w, (name, c0) in enumerate((("cqT", CQ), ("ckvT", CKV))):
                for a in range(TT):
                    b = begin(name, a)
                    pe.wait_ge(c_normed, 2 * w + a + 1)
                    for t in range(4):
                        ins = pe.transpose(b[:, t * P:(t + 1) * P], H[:, a, c0 + t:c0 + RANK:4], ident)
                    end(ins)
            b = begin("krT")
            pe.wait_ge(kr_rotated, 1)
            for a in range(TT):
                ins = pe.transpose(b[0:ROPE, a * P:(a + 1) * P], kr_rot[:, a, :], ident)
            end(ins)
            pe.wait_ge(landed[0], 16 * (IN0_FULL + 2))
            pe.wait_ge(bias_in, 16)
            emptied("lrT")
            for a in range(TT):
                b = begin("z", a)
                ins = pe.matmul(b[:], lrT[0:GRANK + 1, a * P:(a + 1) * P], w_land[0:GRANK + 1, 0, 0:NB],
                                start=True, stop=True)
                end(ins)
            emptied("cqT", 1)
            pe.wait_ge(landed[1], 16 * (IN0_FULL + 2))
            for a in range(TT):
                b = begin("qr", a)
                for c in range(4):
                    ins = pe.matmul(b[:], cqT[:, c, a * P:(a + 1) * P], land(1)[:, c, :], start=c == 0, stop=c == 3)
                end(ins)

            def per_head(name, i, slot, rhs):
                b = begin(name, i)
                for k in range(2):
                    h = (2 * i + k) % 4
                    for c in range(4):
                        ins = pe.matmul(b[:, k * SEQ:(k + 1) * SEQ], land(slot)[:, c, h * P:(h + 1) * P], rhs[:, c, :],
                                        start=c == 0, stop=c == 3)
                end(ins)

            for i in range(4):
                if i % 2 == 0:
                    pe.wait_ge(landed[2 + i // 2], 16 * (IN0_FULL + 2))
                per_head("qn", i, 2 + i // 2, cqT)
            for a in range(TT):
                b = begin("suf", a)
                pe.wait_ge(logg_ready, a + 1)
                end(pe.matmul(b[:], cst("suffix"), lg[:, a, :], start=True, stop=True))
            b = begin("dec")
            for a in range(TT):
                for h in range(GH):
                    ins = pe.matmul(b[:, 2 * (TT * h + a):2 * (TT * h + a) + 2], lg[:, a, h * GDK:(h + 1) * GDK],
                                    cst("chunk_of"), start=True, stop=True)
            end(ins)
            pe.wait_ge(kdec_ready, TT)
            for i in range(8):
                b = begin("upd", i)
                for k in range(2):
                    c, h = (2 * i + k) // GH, (2 * i + k) % GH
                    r = slice(CHUNK * (c % 2), CHUNK * (c % 2) + CHUNK)
                    ins = pe.matmul(b[:, k * GDV:(k + 1) * GDV], kdec[r, c // 2, h * GDK:(h + 1) * GDK],
                                    H[r, c // 2, GV + h * GDV:GV + (h + 1) * GDV], start=True, stop=True)
                end(ins)
            emptied("ckvT", 1)
            for i in range(4):
                if i % 2 == 0:
                    pe.wait_ge(landed[i // 2], 16 * (IN0_FULL + 3))
                per_head("kn", i, i // 2, ckvT)
            for i in range(4):
                half, a = i // 2, i % 2
                if a == 0:
                    pe.wait_ge(landed[2 + half], 16 * (IN0_FULL + 3))
                b = begin("v", i)
                for c in range(4):
                    ins = pe.matmul(b[:], ckvT[:, c, a * P:(a + 1) * P], land(2 + half)[:, c, :],
                                    start=c == 0, stop=c == 3)
                end(ins)
            for i in range(4):
                a, q = i // 2, i % 2
                b = begin("qrT", i)
                pe.wait_ge(qr_rotated, a + 1)
                for k in range(4):
                    ins = pe.transpose(b[0:ROPE, k * P:(k + 1) * P], qrr[:, a, 4 * q + k, :], ident)
                end(ins)
            emptied("upd", 7)
            emptied("gqT", 1)
            for i in range(4):
                a, q = i // 2, i % 2
                b = begin("ob", i)
                for k in range(2):
                    h = 2 * q + k
                    for cc in range(2):
                        s = slice(a * P + cc * CHUNK, a * P + (cc + 1) * CHUNK)
                        ins = pe.matmul(b[cc * CHUNK:(cc + 1) * CHUNK, k * GDV:(k + 1) * GDV], gqT[:, h, s],
                                        states[:, h, 2 * a + cc, :], start=True, stop=True)
                end(ins)
            emptied("kn", 3)
            emptied("qrT", 3)
            emptied("v", 3)
            for i in range(6):
                a = 0 if i < 2 else 1
                keys = P * (a + 1)
                per = NB // keys
                h0 = i * 4 if a == 0 else (i - 2) * 2
                b = begin("s", i)
                for k in range(per):
                    h = h0 + k
                    dst = b[:, k * keys:(k + 1) * keys]
                    pe.matmul(dst, qnT[:, h, a * P:(a + 1) * P], knT[:, h, 0:keys], start=True, stop=False)
                    ins = pe.matmul(dst, qrT[:, h, a * P:(a + 1) * P], krT[:, 0:keys], start=False, stop=True)
                end(ins)
            for i in range(6):
                b = begin("pT", i)
                pe.wait_ge(p_ready, 1 if i < 2 else 2)
                for k in range(4):
                    if i < 2:
                        src = S0[:, 4 * i + k, :]
                    else:
                        m = 4 * (i - 2) + k
                        src = S1[:, m // 2, (m % 2) * P:(m % 2 + 1) * P]
                    ins = pe.transpose(b[:, k * P:(k + 1) * P], src, ident)
                end(ins)
            emptied("pT", 5)
            for i in range(4):
                a, q = i // 2, i % 2
                b = begin("o", i)
                for k in range(4):
                    h = 4 * q + k
                    for kb in range(a + 1):
                        pt = pT0[:, h, :] if a == 0 else pT1[:, h, kb, :]
                        ins = pe.matmul(b[:, k * P:(k + 1) * P], pt, vv[:, kb, h * VD:(h + 1) * VD],
                                        start=kb == 0, stop=kb == a)
                end(ins)
            emptied("o", 3)
            transposes(T_OUT0, lambda a, t: H[:, a, (0, GV)[t // 8] + t % 8:(0, GV)[t // 8] + 1024:8], lambda a, q: None)
            pe.wait_ge(t_low, T_OUT0 + 8)

            def out_projection(sb0, ev0):
                for b in range(NBLK):
                    if b >= 2:
                        pe.wait_ge(gemm_out_v, ev0 + 2 * (b - 1))
                    gemm_block(sb0 + b, b % 2)

            out_projection(SB_OUT0, IN0_FULL + 1)

            def route_tokens(layer):
                t0 = (T_R0, T_R1)[layer]
                if layer == 0:
                    pe.wait_ge(rw_split, 1)

                def logits(g):
                    a, q = g // 4, g % 4
                    pe.wait_ge(t_low, t0 + g + 1)
                    for c in range(4):
                        t = 4 * q + c
                        ins = three(bank[6 + a][:, 0:NEXP], rt_hi[:, g % 2, c, :], rt_lo[:, g % 2, c, :],
                                    rw_hi[:, t, :], rw_lo[:, t, :], t == 0, t == KT - 1)
                    if q == 3:
                        ins.then_inc(logits_done, 1)

                for g in range(8):
                    a, q = g // 4, g % 4
                    pe.wait_ge(x_ready, (2 * layer) * 8 + 4 * (a + 1))
                    if g >= 2:
                        pe.wait_ge(t_low, t0 + g - 1)
                    for c in range(4):
                        t = 4 * q + c
                        ins = pe.transpose(bank[4 + g % 2][:, c * P:(c + 1) * P], X[:, a, t:D:KT], ident)
                    ins.then_inc(t_filled, 1)
                    if g:
                        logits(g - 1)
                logits(7)
                pe.wait_ge(sel_ready, layer + 1)
                sel = route[:, 15]
                for a in range(TT):
                    dst = bank[6][:, 64 + 32 * a:64 + 32 * a + NEXP]
                    if a:
                        pe.matmul(dst, cst("ones"), sel[:, 0, :], start=True, stop=False)
                    pe.matmul(dst, cst("lower"), sel[:, a, :], start=a == 0, stop=True)
                for a in range(TT):
                    ins = pe.matmul(bank[6][:, 128:128 + NEXP], cst("ones"), sel[:, a, :], start=a == 0, stop=a == 1)
                ins.then_inc(rank_done, 1)

            def gather(s, pair, groups):
                for q, part in [(q, part) for q in groups for part in range(2)]:
                    src = (x_hi, x_lo)[part]
                    dst = bank[4 + 2 * (q % 2) + part]
                    ge(pe, (s.xg_out_h, s.xg_out_l)[part], 8 * pair + q - 1)
                    for c in range(2):
                        t = 2 * q + c
                        for a in range(TT):
                            ins = pe.matmul(dst[:, c * 2 * CAP:(c + 1) * 2 * CAP], src[:, a, t:D:KT],
                                            place_r[:, a, :], start=a == 0, stop=a == TT - 1)
                    ins.then_inc((s.xg_fill_h, s.xg_fill_l)[part], 1)

            def scatter(s, m, half, gathered):
                pe.wait_ge(s.y_lo_done, m + 1)
                ge(pe, s.acc_done, m)
                ge(pe, s.xg_out_h, gathered)
                ge(pe, s.xg_out_l, gathered)
                for a in range(TT):
                    pe.matmul(bank[6 + a][:], placeT[:, a * P:(a + 1) * P], y_hi[:, half, :], start=True, stop=False)
                    ins = pe.matmul(bank[6 + a][:], placeT[:, a * P:(a + 1) * P], y_lo[:, half, :],
                                    start=False, stop=True)
                ins.then_inc(s.scat_fill, 1)

            def experts(layer, s, sb0, p0):
                pe.wait_ge(s.place_r_ready, p0 + 1)
                gather(s, p0, range(8))

                def body(p, first, last):
                    pair, B = p0 + p, sb0 + 6 * p

                    def up_gate(b, k, part, js):
                        for j in js:
                            pe.wait_ge(s.lo_done[j], B + b + 1)
                            for c in range(4):
                                t = 4 * j + c
                                ins = three(bank[part][:], xg_hi[:, t, k * CAP:(k + 1) * CAP],
                                            xg_lo[:, t, k * CAP:(k + 1) * CAP], hi(j)[:, c, :], lo(j)[:, c, :],
                                            t == 0, t == KT - 1)
                            ins.then_inc(s.used, 1)

                    def slots(E):
                        pe.wait_ge(s.place_ready, E + 1)
                        for a in range(TT):
                            ins = pe.transpose(bank[2][:, a * P:(a + 1) * P], place[:, a, :], ident)
                        ins.then_inc(s.pt_fill, 1)

                    def hidden(E):
                        pe.wait_ge(s.h_done, E + 1)
                        for c in range(4):
                            ins = pe.transpose(bank[3][:, c * P:(c + 1) * P], hid[:, c:DEXP:4], ident)
                        ins.then_inc(s.hT_fill, 1)

                    def down(b, E, gathered):
                        for n in range(4):
                            pe.wait_ge(s.lo_done[n], B + b + 1)
                            if n == 0:
                                pe.wait_ge(s.hT_lo_done, E + 1)
                                pe.wait_ge(s.pt_done, E + 1)
                            if n >= 2:
                                pe.wait_ge(s.y_lo_done, 4 * E + n - 1)
                            for c in range(4):
                                ins = three(bank[2 + n % 2][:], hT_hi[:, c, :], hT_lo[:, c, :], hi(n)[:, c, :],
                                            lo(n)[:, c, :], c == 0, c == 3)
                            ins.then_inc(s.used, 1)
                            if n:
                                scatter(s, 4 * E + n - 1, (n - 1) % 2, gathered)

                    E0, E1 = 2 * pair, 2 * pair + 1
                    pe.wait_ge(s.xg_out_h, 8 * (pair + 1))
                    pe.wait_ge(s.xg_out_l, 8 * (pair + 1))
                    ge(pe, s.silu_done, E0)
                    up_gate(0, 0, 0, [0])
                    if not first:
                        scatter(s, 4 * E0 - 1, 1, 8 * (pair + 1))
                    up_gate(0, 0, 0, [1, 2, 3])
                    ge(pe, s.h_done, E0)
                    up_gate(1, 0, 1, range(4))
                    pe.wait_ge(s.silu_done, E0 + 1)
                    up_gate(2, 1, 0, [0, 1])
                    slots(E0)
                    hidden(E0)
                    up_gate(2, 1, 0, [2, 3])
                    down(3, E0, 8 * (pair + 1))
                    up_gate(4, 1, 1, [0])
                    scatter(s, 4 * E0 + 3, 1, 8 * (pair + 1))
                    up_gate(4, 1, 1, [1])
                    if not last:
                        pe.wait_ge(s.place_r_ready, pair + 2)
                        pe.wait_ge(s.acc_done, 4 * E1)
                        gather(s, pair + 1, [0, 1])
                    up_gate(4, 1, 1, [2])
                    if not last:
                        gather(s, pair + 1, [2, 3])
                    up_gate(4, 1, 1, [3])
                    slots(E1)
                    if not last:
                        gather(s, pair + 1, [4, 5])
                    hidden(E1)
                    if not last:
                        gather(s, pair + 1, [6, 7])
                    down(5, E1, 8 * (pair + (1 if last else 2)))
                    if last:
                        scatter(s, 4 * E1 + 3, 1, 8 * (pair + 1))
                over_pairs(pe, body)

            def moe(layer):
                route_tokens(layer)
                pe.wait_ge(x_low, 8 * (layer + 1))
                experts(layer, main, (SB_MOE0, SB_MOE1)[layer], layer * NPAIR)
                pe.wait_ge(flag_ready, layer + 1)
                many = pe.value_load(flag[0:1, layer:layer + 1])
                with pe.If(many > CAP):
                    pe.wait_ge(main.acc_done, 4 * NEXP * (layer + 1))
                    experts(layer, overflow[layer], 0, 0)

            moe(0)
            transposes(T_IN1, lambda a, t: X[:, a, t:D:KT],
                       lambda a, q: pe.wait_ge(x_ready, 8 + 4 * (a + 1)))
            pe.wait_ge(t_low, T_IN1 + 8)
            gemm_block(SB_IN1, 0)
            gemm_block(SB_IN1 + 1, 1)
            with pe.Fori(1, 4) as i:
                for p in range(2):
                    pe.wait_ge(gemm_out_a, IN0_FULL + 1 + 2 * (2 * i + p - 1))
                    gemm_block(SB_IN1 + 2 * i + p, p)
            pe.wait_ge(ws_in, 32)
            for i in range(4):
                if i >= 2:
                    pe.wait_ge(wsT_copied, i - 1)
                for k in range(4):
                    ins = pe.transpose(bank[4 + i % 2][:, k * P:(k + 1) * P], ws[:, 4 * i + k, :], ident)
                ins.then_inc(sgu_filled, 1)
            pe.transpose(bank[6][:, 0:GROUPS], bs[:, :], const[0:GROUPS, 0:GROUPS]).then_inc(sgu_filled, 1)
            pe.wait_ge(wsT_ready, 1)
            pe.wait_ge(v_ready, 8)
            pe.wait_ge(gemm_out_a, IN0_FULL + 1 + 16)
            for i in range(8):
                if i >= 4:
                    pe.wait_ge(sgu_out, i - 3)
                for k in range(2):
                    g = 2 * i + k
                    ins = pe.matmul(bank[i % 4][:, k * 2 * P:(k + 1) * 2 * P].rearrange("p (a c) -> p a c", a=TT),
                                    wsT[:, g, :], V[:, :, g * P:(g + 1) * P], start=True, stop=True)
                ins.then_inc(sgu_filled, 1)
            pe.wait_ge(sgu_out, 8)
            transposes(T_OUT1, lambda a, t: U[:, a, t:D:KT], lambda a, q: None)
            pe.wait_ge(t_low, T_OUT1 + 8)
            out_projection(SB_OUT1, IN0_FULL + 1 + 8)
            moe(1)

        @block.scalar
        def _(act):
            chain = Chain(act, chain_a)

            def split(sb, lb, s=main, n=NB, js=range(4)):
                for j in js:
                    act.wait_ge(s.landed[j], 16 * (lb + 1))
                    ge(act, s.used, 4 * (sb - 1) + j + 1)
                    act.copy(w_hi[:, j, 0:4 * n], w_land[:, j, 0:4 * n]).then_inc(s.hi_done, 1)

            def transposed(t0, dst):
                for g in range(8):
                    act.wait_ge(t_filled, t0 + g + 1)
                    act.copy(dst(g), bank[4 + g % 2][:].rearrange("p (c s) -> p c s", c=4)).then_inc(t_high, 1)

            def xT_group(g):
                a, q = g // 4, g % 4
                return xT_hi[:, 4 * q:4 * q + 4, a * P:(a + 1) * P]

            def layer_norm(k):
                act.wait_ge(ln_recip, k + 1)
                act.activation(rstd, inv_var, ACT.Sqrt).then_inc(ln_root, 1)
                act.wait_ge(ln_shift, k + 1)
                for a in range(TT):
                    for n in range(NBLK):
                        v = (V if k == 2 else X)[:, a, n * NB:(n + 1) * NB]
                        act.activation(v, v, ACT.Identity, bias=shift[:, a:a + 1], scale=rstd[:, a:a + 1]) \
                            .then_inc(ln_scaled, 1)

            act.wait_ge(const_in, 16 * 7)
            act.copy(rw_hi[:], rw_land[:]).then_inc(rw_high, 1)
            act.wait_ge(trig_ready, 1)
            act.activation(sinT[:], ropet[:, 0], ACT.Sin).then_inc(trig_done, 1)
            act.activation(cosT[:], ropet[:, 1], ACT.Sin).then_inc(trig_done, 1)
            transposed(T_IN0, xT_group)
            split(0, 0)

            def in0_out(b, half, n=NB):
                act.wait_ge(main.used, 4 * b + 4)
                act.copy(H[:, 0, bass.ds(b * NB, n)], bank[2 * half][:, 0:n]).then_inc(gemm_out_a, 1)

            with act.Fori(0, IN0_FULL // 2 - 1) as i:
                for p in range(2):
                    split(2 * i + p + 1, 2 * i + p + 1)
                    in0_out(2 * i + p, p)
            split(IN0_FULL - 1, IN0_FULL - 1)
            in0_out(IN0_FULL - 2, 0)
            split(IN0_FULL, IN0_FULL, n=W_IN - IN0_FULL * NB)
            in0_out(IN0_FULL - 1, 1)
            in0_out(IN0_FULL, 0, W_IN - IN0_FULL * NB)
            act.wait_ge(gemm_out_a, IN0_FULL + 1)
            act.wait_ge(gemm_out_v, IN0_FULL + 1)

            def filled(name, i=0):
                act.wait_ge(att_filled, FILL_AT[(name, i)] + 1)
                return bank[FILL_AT[(name, i)] % 8]

            def out_(ins):
                ins.then_inc(att_out_a, 1)

            for w in range(2):
                for a in range(TT):
                    ge(act, rms_sq, 2 * w + a - 1)
                    act.activation(la[:, a, :], H[:, a, w * RANK:(w + 1) * RANK], ACT.Square,
                                   accum_out=att[:, 2 * w + a:2 * w + a + 1]).then_inc(rms_sq, 1)
            act.wait_ge(rms_rec, 1)
            act.activation(att[:, 8:12], att[:, 4:8], ACT.Sqrt).then_inc(rms_root, 1)
            for a in range(TT):
                b = filled("gqT", a)
                out_(act.mul(gqT[:, :, a * P:(a + 1) * P], b[:].rearrange("p (h s) -> p h s", h=GH), GDK ** -0.5))
            b = filled("lrT")
            act.wait_ge(ones_set, 1)
            out_(act.copy(lrT[0:GRANK, :], b[0:GRANK, 0:SEQ]))
            b = filled("krT")
            out_(act.copy(krT[:, :], b[0:ROPE, 0:SEQ]))
            for a in range(TT):
                b = filled("z", a)
                chain(act.activation(la[:, a, :], b[:], ACT.Abs))
                chain.wait()
                chain(act.activation(la[:, a, :], la[:, a, :], ACT.Exp, scale=-1.0))
                chain.wait()
                act.activation(la[:, a, :], la[:, a, :], ACT.Ln, bias=1.0).then_inc(z_soft, 1)
            for i in range(4):
                b = filled("qn", i)
                out_(act.copy(qnT[:, 2 * i:2 * i + 2, :], b[:].rearrange("p (h s) -> p h s", h=2)))
            for a in range(TT):
                b = filled("suf", a)
                out_(act.activation(la[:, a, :], b[:], ACT.Exp))
            b = filled("dec")
            out_(act.activation(dec[:].rearrange("p h c -> p (h c)"), b[:, 0:GH * 4], ACT.Exp))
            for i in range(4):
                b = filled("kn", i)
                out_(act.copy(knT[:, 2 * i:2 * i + 2, :], b[:].rearrange("p (h s) -> p h s", h=2)))
            for i in range(4):
                b = filled("v", i)
                half, a = i // 2, i % 2
                out_(act.copy(vv[:, a, half * NB:(half + 1) * NB], b[:]))
            for i in range(4):
                b = filled("qrT", i)
                a, q = i // 2, i % 2
                out_(act.copy(qrT[:, 4 * q:4 * q + 4, a * P:(a + 1) * P],
                              b[0:ROPE, :].rearrange("p (h s) -> p h s", h=4)))
            for a in range(TT):
                v = H[:, a, GO:W_IN]
                act.activation(v, v, ACT.Silu).then_inc(go_silu, 1)
            for i in range(4):
                b = filled("ob", i)
                a, q = i // 2, i % 2
                for k in range(2):
                    m = GH * a + 2 * q + k
                    ge(act, ob_sq, m - 1)
                    act.activation(lg[:, 0, (m % 2) * GDV:(m % 2 + 1) * GDV], b[:, k * GDV:(k + 1) * GDV], ACT.Square,
                                   accum_out=att[:, 16 + m:17 + m]).then_inc(ob_sq, 1)
                if q:
                    act.wait_ge(ob_rec, a + 1)
                    act.activation(att[:, 32 + GH * a:32 + GH * (a + 1)], att[:, 24 + GH * a:24 + GH * (a + 1)],
                                   ACT.Sqrt).then_inc(ob_root, 1)
            for i in range(6):
                b = filled("s", i)
                if i < 2:
                    dst = S0[:, 4 * i:4 * i + 4, :]
                else:
                    dst = S1[:, 2 * (i - 2):2 * (i - 2) + 2, :]
                out_(act.mul(dst, b[:].rearrange("p (h s) -> p h s", h=dst.shape[1]), (NOPE + ROPE) ** -0.5))
            for a, S in enumerate((S0, S1)):
                act.wait_ge(s_shifted, a + 1)
                act.activation(S[:], S[:], ACT.Exp).then_inc(p_ready, 1)
            for i in range(6):
                b = filled("pT", i)
                if i < 2:
                    dst = pT0[:, 4 * i:4 * i + 4, :]
                else:
                    dst = pT1[:, 2 * (i - 2):2 * (i - 2) + 2, :, :].rearrange("p h k s -> p (h k) s")
                out_(act.copy(dst, b[:].rearrange("p (h s) -> p h s", h=4)))

            transposed(T_OUT0, xT_group)
            for b in range(NBLK):
                split(SB_OUT0 + b, land_block(SB_OUT0 + b))

            def tokens_out(s, pair, qs, used=None):
                for q in qs:
                    act.wait_ge(s.xg_fill_h, 8 * pair + q + 1)
                    if used is not None:
                        act.wait_ge(s.used, used + q // 2 + 1)
                    act.copy(xg_hi[:, 2 * q:2 * q + 2, :], bank[4 + 2 * (q % 2)][:].rearrange("p (c s) -> p c s", c=2)) \
                        .then_inc(s.xg_out_h, 1)

            def experts(s, sb0, p0, lb0):
                split(sb0, lb0, s)
                tokens_out(s, p0, range(8))

                def body(p, first, last):
                    pair, B, L = p0 + p, sb0 + 6 * p, lb0 + 6 * p
                    E0, E1 = 2 * pair, 2 * pair + 1

                    def ahead(b, js=range(4)):
                        split(B + b, L + b, s, js=js)

                    def silu(E, b):
                        act.wait_ge(s.used, 4 * (B + b) + 4)
                        ge(act, s.h_done, E)
                        act.activation(gsil[:], bank[0][:], ACT.Silu).then_inc(s.silu_done, 1)

                    def slots(E):
                        act.wait_ge(s.pt_fill, E + 1)
                        act.copy(placeT[:], bank[2][:, 0:SEQ]).then_inc(s.pt_done, 1)

                    def hidden(E):
                        act.wait_ge(s.hT_fill, E + 1)
                        act.copy(hT_hi[:], bank[3][:].rearrange("p (c s) -> p c s", c=4)).then_inc(s.hT_hi_done, 1)

                    def y_out(E, b, n):
                        act.wait_ge(s.used, 4 * (B + b) + n + 1)
                        ge(act, s.scat_fill, 4 * E + n - 1)
                        act.copy(y_hi[:, n % 2, :], bank[2 + n % 2][:]).then_inc(s.y_hi_done, 1)

                    ahead(1)
                    silu(E0, 0)
                    ahead(2)
                    ahead(3, [0, 1])
                    slots(E0)
                    hidden(E0)
                    ahead(3, [2, 3])
                    silu(E1, 2)
                    for n in range(4):
                        y_out(E0, 3, n)
                        ahead(4, [n])
                    ahead(5, [0, 1])
                    if not last:
                        tokens_out(s, pair + 1, [0, 1], 4 * (B + 4))
                    ahead(5, [2])
                    if not last:
                        tokens_out(s, pair + 1, [2, 3], 4 * (B + 4))
                    slots(E1)
                    if not last:
                        tokens_out(s, pair + 1, [4, 5], 4 * (B + 4))
                    hidden(E1)
                    if not last:
                        tokens_out(s, pair + 1, [6, 7], 4 * (B + 4))
                    ahead(5, [3])
                    for n in range(4):
                        y_out(E1, 5, n)
                        if not last:
                            ahead(6, [n])
                over_pairs(act, body)

            def moe(layer):
                layer_norm((0, 3)[layer])
                for k in range(TT * NBLK):
                    a, n = k // NBLK, k % NBLK
                    act.wait_ge(x_ready, 16 * layer + k + 1)
                    act.copy(x_hi[:, a, n * NB:(n + 1) * NB], X[:, a, n * NB:(n + 1) * NB]).then_inc(x_high, 1)
                transposed((T_R0, T_R1)[layer], lambda g: rt_hi[:, g % 2])
                for a in range(TT):
                    act.wait_ge(logits_done, 2 * layer + a + 1)
                    act.activation(route[:, 0, a, :], bank[6 + a][:, 0:NEXP], ACT.Sigmoid).then_inc(sigm_done, 1)
                sb0 = (SB_MOE0, SB_MOE1)[layer]
                experts(main, sb0, layer * NPAIR, land_block(sb0))
                act.wait_ge(flag_ready, layer + 1)
                many = act.value_load(flag[0:1, layer:layer + 1])
                with act.If(many > CAP):
                    act.wait_ge(main.used, 4 * (sb0 + 3 * NEXP))
                    act.wait_ge(main.scat_fill, 4 * NEXP * (layer + 1))
                    experts(overflow[layer], 0, 0, 0)
                layer_norm((1, 4)[layer])

            moe(0)
            transposed(T_IN1, xT_group)
            lb1 = land_block(SB_IN1)
            split(SB_IN1, lb1)

            def in1_out(b, half):
                act.wait_ge(main.used, 4 * (SB_IN1 + b) + 4)
                for a in range(TT):
                    act.activation(UV[:, a, bass.ds(b * NB, NB)], bank[2 * half + a][:], ACT.Gelu_apprx_tanh) \
                        .then_inc(gemm_out_a, 1)

            with act.Fori(0, 3) as i:
                for p in range(2):
                    split(SB_IN1 + 2 * i + p + 1, lb1 + 2 * i + p + 1)
                    in1_out(2 * i + p, p)
            split(SB_IN1 + 7, lb1 + 7)
            in1_out(6, 0)
            split(SB_OUT1, lb1 + 8)
            in1_out(7, 1)
            act.wait_ge(gemm_out_a, IN0_FULL + 1 + 16)
            layer_norm(2)
            for i in range(4):
                act.wait_ge(sgu_filled, i + 1)
                act.copy(wsT[:, 4 * i:4 * i + 4, :], bank[4 + i % 2][:].rearrange("p (g s) -> p g s", g=4)) \
                    .then_inc(wsT_copied, 1)
            act.wait_ge(sgu_filled, 5)
            act.copy(bsT[:], bank[6][:, 0:GROUPS]).then_inc(wsT_copied, 1)
            transposed(T_OUT1, xT_group)
            for b in range(1, NBLK):
                split(SB_OUT1 + b, land_block(SB_OUT1 + b))
            moe(1)

        @block.vector
        def _(dve):
            chain = Chain(dve, chain_v)

            def split(sb, s=main, n=NB, js=range(4)):
                for j in js:
                    dve.wait_ge(s.hi_done, 4 * sb + j + 1)
                    dve.tensor_tensor(w_lo[:, j, 0:4 * n], w_land[:, j, 0:4 * n], w_hi[:, j, 0:4 * n], ALU.subtract) \
                        .then_inc(s.lo_done[j], 1)

            def transposed(t0, high, low):
                for g in range(8):
                    dve.wait_ge(t_high, t0 + g + 1)
                    dve.tensor_tensor(low(g), bank[4 + g % 2][:].rearrange("p (c s) -> p c s", c=4), high(g),
                                      ALU.subtract).then_inc(t_low, 1)

            def group_of(x):
                return lambda g: x[:, 4 * (g % 4):4 * (g % 4) + 4, (g // 4) * P:(g // 4 + 1) * P]

            def block_stats(x, a, n):
                chain(dve.bn_stats(stats[:, a, n, :], x[:, a, n * NB:(n + 1) * NB]))

            def layer_norm(k, x, signal):
                chain.wait()
                for a in range(TT):
                    chain(dve.bn_aggr(meanvar[:, a, :], stats[:, a].rearrange("p n s -> p (n s)")))
                chain.wait()
                chain(dve.tensor_scalar(inv_var, meanvar[:, :, 1], EPS, None, ALU.add))
                chain.wait()
                dve.reciprocal(inv_var, inv_var).then_inc(ln_recip, 1)
                dve.wait_ge(ln_root, k + 1)
                dve.scalar_tensor_tensor(shift, meanvar[:, :, 0], -1.0, rstd, ALU.mult, ALU.mult) \
                    .then_inc(ln_shift, 1)
                dve.wait_ge(rows_in, 32 * (k + 1))
                views = [(x[:, m // NBLK, (m % NBLK) * NB:(m % NBLK + 1) * NB],
                          rows[:, 0, (m % NBLK) * NB:(m % NBLK + 1) * NB],
                          rows[:, 1, (m % NBLK) * NB:(m % NBLK + 1) * NB]) for m in range(TT * NBLK)]
                for m in range(TT * NBLK + 1):
                    if m < TT * NBLK:
                        v, g, _ = views[m]
                        dve.wait_ge(ln_scaled, TT * NBLK * k + m + 1)
                        chain(dve.tensor_tensor(v, v, g, ALU.mult))
                    if m:
                        v, _, b = views[m - 1]
                        dve.wait_ge(chain_v, chain.n - (1 if m < TT * NBLK else 0))
                        dve.tensor_tensor(v, v, b, ALU.add).then_inc(signal, 1)
                dve.wait_ge(signal, {0: 8, 1: 16, 2: 8, 3: 24, 4: 32}[k])
                dve.sem_inc(rows_used, 1)

            dve.wait_ge(const_in, 16 * 7)
            chain(dve.tensor_copy(posf[:], posi[:]))
            chain.wait()
            for a in range(TT):
                chain(dve.tensor_scalar(ropet[:, 2, a, :], cst("inv_freq"), posf[:, a:a + 1], None, ALU.mult))
            chain.wait()
            ang, sarg, carg, tmp = (ropet[:, i] for i in (2, 0, 1, 3))
            chain(dve.tensor_scalar(tmp, ang, 1.0 / (2 * np.pi), ROUND, ALU.mult, ALU.add))
            chain.wait()
            chain(dve.tensor_scalar(tmp, tmp, -ROUND, None, ALU.add))
            chain.wait()
            for i, part in enumerate((C2PI_A, C2PI_B, C2PI_C)):
                chain(dve.scalar_tensor_tensor(sarg, tmp, -part, sarg if i else ang, ALU.mult, ALU.add))
                chain.wait()

            def wrap(v):
                for limit, op, back in ((np.pi, ALU.is_gt, -2 * np.pi), (-np.pi, ALU.is_lt, 2 * np.pi)):
                    chain(dve.tensor_scalar(tmp, v, float(limit), float(back), op, ALU.mult))
                    chain.wait()
                    chain(dve.tensor_tensor(v, v, tmp, ALU.add))
                    chain.wait()

            wrap(sarg)
            chain(dve.tensor_scalar(carg, sarg, float(np.pi / 2), None, ALU.add))
            chain.wait()
            wrap(carg)
            chain(dve.tensor_scalar(sarg, sarg, PI_IN, -PI_IN, ALU.min, ALU.max))
            dve.tensor_scalar(carg, carg, PI_IN, -PI_IN, ALU.min, ALU.max).then_inc(trig_ready, 1)
            dve.wait_ge(rw_high, 1)
            dve.tensor_tensor(rw_lo[:], rw_land[:], rw_hi[:], ALU.subtract).then_inc(rw_split, 1)

            transposed(T_IN0, group_of(xT_hi), group_of(xT_lo))
            split(0)

            def in0_out(b, half, n=NB):
                dve.wait_ge(main.used, 4 * b + 4)
                dve.tensor_copy(H[:, 1, bass.ds(b * NB, n)], bank[2 * half + 1][:, 0:n]).then_inc(gemm_out_v, 1)

            with dve.Fori(0, IN0_FULL // 2 - 1) as i:
                for p in range(2):
                    split(2 * i + p + 1)
                    in0_out(2 * i + p, p)
            split(IN0_FULL - 1)
            in0_out(IN0_FULL - 2, 0)
            split(IN0_FULL, n=W_IN - IN0_FULL * NB)
            in0_out(IN0_FULL - 1, 1)
            in0_out(IN0_FULL, 0, W_IN - IN0_FULL * NB)
            dve.memset(lrT[:], 1.0).then_inc(ones_set, 1)
            dve.wait_ge(gemm_out_a, IN0_FULL + 1)
            dve.wait_ge(gemm_out_v, IN0_FULL + 1)

            def filled(name, i=0):
                dve.wait_ge(att_filled, FILL_AT[(name, i)] + 1)
                return bank[FILL_AT[(name, i)] % 8]

            def out_(ins):
                ins.then_inc(att_out_v, 1)

            def heads_of(x, n):
                return x.unsqueeze(1).to_broadcast([P, n, x.shape[1]])

            dve.wait_ge(trig_done, 2)
            k1, k2 = H[:, :, KR:KR + HALF], H[:, :, KR + HALF:KR + ROPE]
            chain(dve.tensor_tensor(ropet[:, 0], k1, cosT[:], ALU.mult))
            chain(dve.tensor_tensor(ropet[:, 1], k2, sinT[:], ALU.mult))
            chain(dve.tensor_tensor(ropet[:, 2], k2, cosT[:], ALU.mult))
            chain(dve.tensor_tensor(ropet[:, 3], k1, sinT[:], ALU.mult))
            chain.wait()
            chain(dve.tensor_tensor(kr_rot[:, :, 0:HALF], ropet[:, 0], ropet[:, 1], ALU.subtract))
            dve.tensor_tensor(kr_rot[:, :, HALF:ROPE], ropet[:, 2], ropet[:, 3], ALU.add).then_inc(kr_rotated, 1)
            dve.wait_ge(rms_sq, 4)
            chain(dve.tensor_scalar(att[:, 4:8], att[:, 0:4], 1.0 / RANK, EPS, ALU.mult, ALU.add))
            chain.wait()
            dve.reciprocal(att[:, 4:8], att[:, 4:8]).then_inc(rms_rec, 1)
            dve.wait_ge(rms_root, 1)
            for w in range(2):
                for a in range(TT):
                    v = H[:, a, w * RANK:(w + 1) * RANK]
                    dve.tensor_scalar(v, v, att[:, 8 + 2 * w + a:9 + 2 * w + a], None, ALU.mult) \
                        .then_inc(c_normed, 1)
            for w, (name, dst) in enumerate((("cqT", cqT), ("ckvT", ckvT))):
                for a in range(TT):
                    b = filled(name, a)
                    out_(dve.tensor_tensor(dst[:, :, a * P:(a + 1) * P], b[:].rearrange("p (c s) -> p c s", c=4),
                                           gains[:, w, :].unsqueeze(2).to_broadcast([P, 4, P]), ALU.mult))
            for a in range(TT):
                b = filled("z", a)
                dve.wait_ge(z_soft, a + 1)
                out_(dve.scalar_tensor_tensor(lg[:, a, :], b[:], 0.0, la[:, a, :], ALU.min, ALU.subtract))
                dve.wait_ge(att_out_v, EMPTIED[("z", a)][1])
                dve.sem_inc(logg_ready, 1)
            for a in range(TT):
                b = filled("qr", a)[:].rearrange("p (h d) -> p h d", h=HEADS)
                q1, q2 = b[:, :, 0:HALF], b[:, :, HALF:ROPE]
                cos, sin = heads_of(cosT[:, a, :], HEADS), heads_of(sinT[:, a, :], HEADS)
                chain(dve.tensor_tensor(rtmp[:, 0], q1, cos, ALU.mult))
                chain(dve.tensor_tensor(rtmp[:, 1], q2, sin, ALU.mult))
                chain.wait()
                chain(dve.tensor_tensor(qrr[:, a, :, 0:HALF], rtmp[:, 0], rtmp[:, 1], ALU.subtract))
                chain.wait()
                chain(dve.tensor_tensor(rtmp[:, 0], q2, cos, ALU.mult))
                out_(dve.tensor_tensor(rtmp[:, 1], q1, sin, ALU.mult))
                chain.wait()
                dve.wait_ge(att_out_v, EMPTIED[("qr", a)][1])
                dve.tensor_tensor(qrr[:, a, :, HALF:ROPE], rtmp[:, 0], rtmp[:, 1], ALU.add).then_inc(qr_rotated, 1)
                dve.wait_ge(qr_rotated, a + 1)
            for a in range(TT):
                dve.wait_ge(att_out_a, EMPTIED[("suf", a)][1])
                dve.tensor_tensor(kdec[:, a, :], H[:, a, GK:GK + GH * GDK], la[:, a, :], ALU.mult) \
                    .then_inc(kdec_ready, 1)
            dve.wait_ge(att_out_a, EMPTIED[("dec", 0)][1])
            for i in range(8):
                b = filled("upd", i)
                for k in range(2):
                    c, h = (2 * i + k) // GH, (2 * i + k) % GH
                    upd = b[:, k * GDV:(k + 1) * GDV]
                    if c == 0:
                        ins = dve.tensor_copy(states[:, h, 0, :], upd)
                    else:
                        dve.wait_ge(att_out_v, EMPTIED[("upd", i - 2)][1])
                        dve.wait_ge(chain_v, chain.n)
                        ins = dve.scalar_tensor_tensor(states[:, h, c, :], states[:, h, c - 1, :],
                                                       dec[:, h, c:c + 1], upd, ALU.mult, ALU.add)
                    (out_ if k else chain)(ins)
            for a in range(TT):
                dve.wait_ge(go_silu, a + 1)
                v = H[:, a, GO:W_IN].rearrange("p (h d) -> p h d", h=GH)
                chain(dve.tensor_tensor(v, v, heads_of(gnorm[:], GH), ALU.mult))
            for a in range(TT):
                dve.wait_ge(ob_sq, GH * (a + 1))
                m = att[:, 24 + GH * a:24 + GH * (a + 1)]
                chain(dve.tensor_scalar(m, att[:, 16 + GH * a:16 + GH * (a + 1)], 1.0 / GDV, EPS, ALU.mult, ALU.add))
                chain.wait()
                dve.reciprocal(m, m).then_inc(ob_rec, 1)
                dve.wait_ge(ob_root, a + 1)
                for q in range(2):
                    b = filled("ob", 2 * a + q)
                    for k in range(2):
                        h = 2 * q + k
                        ins = dve.scalar_tensor_tensor(
                            H[:, a, GV + h * GDV:GV + (h + 1) * GDV], b[:, k * GDV:(k + 1) * GDV],
                            att[:, 32 + GH * a + h:33 + GH * a + h], H[:, a, GO + h * GDV:GO + (h + 1) * GDV],
                            ALU.mult, ALU.mult)
                        (out_ if k else chain)(ins)
            for a, S in enumerate((S0, S1)):
                keys = P * (a + 1)
                dve.wait_ge(att_out_a, EMPTIED[("s", (1, 5)[a])][1])
                chain(dve.memset(S[0:CHUNK, :, keys - CHUNK:keys], -BIG))
                chain.wait()
                mx = att[:, 40 + HEADS * a:40 + HEADS * (a + 1)]
                chain(dve.tensor_reduce(mx, S[:], AX_X, ALU.max))
                chain.wait()
                dve.tensor_tensor(S[:], S[:], mx.unsqueeze(2).to_broadcast([P, HEADS, keys]), ALU.subtract) \
                    .then_inc(s_shifted, 1)
            for a, S in enumerate((S0, S1)):
                dve.wait_ge(p_ready, a + 1)
                chain(dve.tensor_reduce(att[:, 56 + HEADS * a:56 + HEADS * (a + 1)], S[:], AX_X, ALU.add))
            chain.wait()
            chain(dve.reciprocal(att[:, 72:88], att[:, 56:72]))
            chain.wait()
            for i in range(4):
                a, q = i // 2, i % 2
                b = filled("o", i)
                r = att[:, 72 + HEADS * a + 4 * q:72 + HEADS * a + 4 * q + 4]
                out_(dve.tensor_tensor(H[:, a, q * NB:(q + 1) * NB].rearrange("p (h d) -> p h d", h=4),
                                       b[:].rearrange("p (h d) -> p h d", h=4),
                                       r.unsqueeze(2).to_broadcast([P, 4, VD]), ALU.mult))

            def out_projection(sb0, ev0):
                for b in range(NBLK):
                    if b + 1 < NBLK:
                        split(sb0 + b + 1)
                    dve.wait_ge(main.used, 4 * (sb0 + b) + 4)
                    for a in range(TT):
                        v = X[:, a, b * NB:(b + 1) * NB]
                        dve.scalar_tensor_tensor(v, v, ALPHA, bank[2 * (b % 2) + a][:], ALU.mult, ALU.add) \
                            .then_inc(gemm_out_v, 1)
                    for a in range(TT):
                        dve.wait_ge(gemm_out_v, ev0 + 2 * b + a + 1)
                        block_stats(X, a, b)

            transposed(T_OUT0, group_of(xT_hi), group_of(xT_lo))
            split(SB_OUT0)
            out_projection(SB_OUT0, IN0_FULL + 1)

            def route_tokens(layer):
                r = [route[:, i] for i in range(16)]
                score, biased, ing, e1, oh1, masked, sel = r[0], r[1], r[2], r[3], r[4], r[5], r[15]
                q = [r[7][:, :, 4 * i:4 * i + 4] for i in range(4)] + [r[8][:, :, 4 * i:4 * i + 4] for i in range(4)]
                one = [r[9][:, :, i:i + 1] for i in range(8)]
                dve.wait_ge(sigm_done, 2 * layer + 2)

                def step(ins):
                    chain(ins)
                    chain.wait()

                def tt(out_ap, x, y, op):
                    step(dve.tensor_tensor(out_ap, x, y, op))

                step(dve.tensor_tensor(biased, score, rbias[:].unsqueeze(1).to_broadcast([P, TT, NEXP]), ALU.add))
                g = biased.rearrange("p a (g e) -> p a g e", g=NGRP)
                a0, a1, a2, a3 = (g[:, :, :, i] for i in range(EPG))
                hi1, lo1, hi2, lo2, top, m1, m2, gs = q
                tt(hi1, a0, a1, ALU.max)
                tt(lo1, a0, a1, ALU.min)
                tt(hi2, a2, a3, ALU.max)
                tt(lo2, a2, a3, ALU.min)
                tt(top, hi1, hi2, ALU.max)
                tt(m1, hi1, hi2, ALU.min)
                tt(m2, lo1, lo2, ALU.max)
                tt(m1, m1, m2, ALU.max)
                tt(gs, top, m1, ALU.add)

                def first_of(x, n, weights, best, onehot, work):
                    step(dve.tensor_reduce(best, x, AX_X, ALU.max))
                    tt(work, x, best.to_broadcast([P, TT, n]), ALU.is_equal)
                    tt(work, work, weights.unsqueeze(1).to_broadcast([P, TT, n]), ALU.mult)
                    step(dve.tensor_reduce(best, work, AX_X, ALU.max))
                    tt(onehot, work, best.to_broadcast([P, TT, n]), ALU.is_equal)

                first_of(gs, NGRP, cst("four"), one[0], hi1, lo1)
                step(dve.tensor_copy(ing.rearrange("p a (g e) -> p a g e", g=NGRP),
                                     hi1.unsqueeze(3).to_broadcast([P, TT, NGRP, EPG])))
                tt(masked, biased, ing, ALU.mult)
                step(dve.tensor_scalar(e1, ing, BIG, -BIG, ALU.mult, ALU.add))
                tt(masked, masked, e1, ALU.add)
                first_of(masked, NEXP, cst("sixteen"), one[1], oh1, e1)
                step(dve.tensor_scalar(e1, oh1, -BIG, None, ALU.mult))
                step(dve.tensor_scalar(r[6], oh1, -1.0, 1.0, ALU.mult, ALU.add))
                tt(masked, masked, r[6], ALU.mult)
                tt(masked, masked, e1, ALU.add)
                first_of(masked, NEXP, cst("sixteen"), one[2], r[10], r[11])
                chain(dve.tensor_tensor(sel, oh1, r[10], ALU.add))
                chain.wait()
                dve.sem_inc(sel_ready, 1)
                tt(r[12], score, sel, ALU.mult)
                step(dve.tensor_reduce(one[3], r[12], AX_X, ALU.add))
                step(dve.reciprocal(one[4], one[3]))
                tt(comb[:], r[12], one[4].to_broadcast([P, TT, NEXP]), ALU.mult)
                step(dve.tensor_scalar(r[13], sel, -FAR, FAR, ALU.mult, ALU.add))
                dve.wait_ge(rank_done, layer + 1)
                step(dve.tensor_reduce(flagf[:, layer:layer + 1], bank[6][:, 128:128 + NEXP], AX_X, ALU.max))
                dve.tensor_copy(flag[:, layer:layer + 1], flagf[:, layer:layer + 1]).then_inc(flag_ready, 1)
                got = bank[6][:, 64:128].rearrange("p (a e) -> p a e", a=TT)[:, :, 0:NEXP]
                dve.tensor_tensor(rank[:], got, r[13], ALU.add).then_inc(rank_ready, 1)

            def tokens_out(s, pair, qs, used=None):
                for q in qs:
                    dve.wait_ge(s.xg_fill_l, 8 * pair + q + 1)
                    if used is not None:
                        dve.wait_ge(s.used, used + q // 2 + 1)
                    dve.tensor_copy(xg_lo[:, 2 * q:2 * q + 2, :], bank[5 + 2 * (q % 2)][:].rearrange("p (c s) -> p c s", c=2)) \
                        .then_inc(s.xg_out_l, 1)

            def experts(s, sb0, p0):
                split(sb0, s)
                tokens_out(s, p0, range(8))

                def add(E, n):
                    m = 4 * E + n
                    dve.wait_ge(s.scat_fill, m + 1)
                    ge(dve, s.acc_done, m - 3)
                    for a in range(TT):
                        v = X[:, a, n * NB:(n + 1) * NB]
                        ins = dve.scalar_tensor_tensor(v, bank[6 + a][:], cur[:, 3, a:a + 1], v, ALU.mult, ALU.add)
                        if a == 0:
                            ins.then_inc(s.acc0_done, 1)
                    ins.then_inc(s.acc_done, 1)

                def body(p, first, last):
                    pair, B = p0 + p, sb0 + 6 * p
                    E0, E1 = 2 * pair, 2 * pair + 1

                    def ahead(b, js=range(4)):
                        split(B + b, s, js=js)

                    def weights(e, E):
                        ge(dve, s.acc_done, 4 * E)
                        dve.tensor_copy(cur[:, 3, :], comb[:, :, bass.ds(e, 1)].rearrange("p a o -> p (a o)")) \
                            .then_inc(s.cur_v, 1)

                    def product(E, b):
                        dve.wait_ge(s.used, 4 * (B + b) + 4)
                        dve.wait_ge(s.silu_done, E + 1)
                        dve.tensor_tensor(hid[:], gsil[:], bank[1][:], ALU.mult).then_inc(s.h_done, 1)

                    def hidden(E):
                        dve.wait_ge(s.hT_hi_done, E + 1)
                        dve.tensor_tensor(hT_lo[:], bank[3][:].rearrange("p (c s) -> p c s", c=4), hT_hi[:],
                                          ALU.subtract).then_inc(s.hT_lo_done, 1)

                    def y_out(E, n):
                        dve.wait_ge(s.y_hi_done, 4 * E + n + 1)
                        dve.tensor_tensor(y_lo[:, n % 2, :], bank[2 + n % 2][:], y_hi[:, n % 2, :], ALU.subtract) \
                            .then_inc(s.y_lo_done, 1)
                        if n:
                            add(E, n - 1)

                    if not first:
                        add(E0 - 1, 3)
                    weights(2 * p, E0)
                    ahead(1)
                    ahead(2, range(3))
                    product(E0, 1)
                    ahead(2, [3])
                    ahead(3, [0, 1])
                    hidden(E0)
                    ahead(3, [2, 3])
                    dve.wait_ge(s.cur_v, E0 + 1)
                    for n in range(4):
                        y_out(E0, n)
                        if n not in POOL_SLOTS:
                            ahead(4, [n])
                    add(E0, 3)
                    weights(2 * p + 1, E1)
                    ahead(5, [0, 1])
                    if not last:
                        tokens_out(s, pair + 1, [0, 1], 4 * (B + 4))
                    ahead(5, [2])
                    if not last:
                        tokens_out(s, pair + 1, [2, 3], 4 * (B + 4))
                    product(E1, 4)
                    if not last:
                        tokens_out(s, pair + 1, [4, 5], 4 * (B + 4))
                    hidden(E1)
                    if not last:
                        tokens_out(s, pair + 1, [6, 7], 4 * (B + 4))
                    ahead(5, [3])
                    dve.wait_ge(s.cur_v, E1 + 1)
                    for n in range(4):
                        y_out(E1, n)
                        if not last and n not in POOL_SLOTS:
                            ahead(6, [n])
                    if last:
                        add(E1, 3)
                over_pairs(dve, body)

            def moe(layer):
                layer_norm((0, 3)[layer], X, x_ready)
                for k in range(TT * NBLK):
                    a, n = k // NBLK, k % NBLK
                    v = slice(n * NB, (n + 1) * NB)
                    dve.wait_ge(x_high, 8 * layer + k + 1)
                    dve.tensor_tensor(x_lo[:, a, v], X[:, a, v], x_hi[:, a, v], ALU.subtract).then_inc(x_low, 1)
                transposed((T_R0, T_R1)[layer], lambda g: rt_hi[:, g % 2], lambda g: rt_lo[:, g % 2])
                route_tokens(layer)
                dve.wait_ge(x_scaled, layer + 1)
                experts(main, (SB_MOE0, SB_MOE1)[layer], layer * NPAIR)
                dve.wait_ge(flag_ready, layer + 1)
                many = dve.value_load(flag[0:1, layer:layer + 1])
                with dve.If(many > CAP):
                    dve.wait_ge(main.acc_done, 4 * NEXP * (layer + 1))
                    experts(overflow[layer], 0, 0)
                    dve.wait_ge(overflow[layer].acc_done, 4 * NEXP)
                    dve.wait_ge(overflow[layer].acc0_done, 4 * NEXP)
                dve.wait_ge(main.acc_done, 4 * NEXP * (layer + 1))
                dve.wait_ge(main.acc0_done, 4 * NEXP * (layer + 1))
                dve.sem_inc(moe_over, 1)
                for n in range(NBLK):
                    for a in range(TT):
                        block_stats(X, a, n)
                layer_norm((1, 4)[layer], X, x_ready)

            moe(0)
            transposed(T_IN1, group_of(xT_hi), group_of(xT_lo))
            for b in range(8):
                split(SB_IN1 + b)
            split(SB_OUT1)
            for n in range(NBLK):
                for a in range(TT):
                    dve.wait_ge(gemm_out_a, IN0_FULL + 1 + 2 * (4 + n) + a + 1)
                    block_stats(V, a, n)
            layer_norm(2, V, v_ready)
            dve.wait_ge(wsT_copied, 5)
            dve.memset(wsT[CHUNK:P, :, 0:CHUNK], 0.0).then_inc(wsT_ready, 1)
            for i in range(8):
                dve.wait_ge(sgu_filled, 5 + i + 1)
                for k in range(2):
                    g = 2 * i + k
                    u = U[:, :, g * P:(g + 1) * P]
                    ins = dve.scalar_tensor_tensor(
                        u, bank[i % 4][:, k * 2 * P:(k + 1) * 2 * P].rearrange("p (a c) -> p a c", a=TT),
                        bsT[:, g:g + 1], u, ALU.add, ALU.mult)
                    if k == 0:
                        chain(ins)
                ins.then_inc(sgu_out, 1)
            transposed(T_OUT1, group_of(xT_hi), group_of(xT_lo))
            out_projection(SB_OUT1, IN0_FULL + 1 + 8)
            moe(1)


_INS = ["x", "positions", "ev_w_in", "ev_q_norm", "ev_kv_norm", "ev_w_uq", "ev_w_ukv", "ev_w_gk2", "ev_b_gk2",
        "ev_gla_norm", "ev_w_out", "od_w_in", "od_sgu_ln_g", "od_sgu_ln_b", "od_w_s", "od_b_s", "od_w_out",
        "ln_mix_g", "ln_mix_b", "ln_ffn_g", "ln_ffn_b", "router_w", "router_b", "moe_w_gate", "moe_w_up", "moe_w_down"]


def kernel(**inputs):
    import concourse.bacc as bacc
    from concourse.bass_utils import run_bass_kernel_spmd

    nc = bacc.Bacc("TRN2", target_bir_lowering=False, num_devices=1)
    arrays, A = {}, {}
    for name in _INS + ["const"]:
        a = np.ascontiguousarray(constants() if name == "const" else inputs[name])
        arrays[f"in_{name}"] = a
        A[name] = nc.dram_tensor(f"in_{name}", a.shape, mybir.dt.from_np(a.dtype), kind="ExternalInput").ap()
    out = nc.dram_tensor("out_x", (1, SEQ, D), F32, kind="ExternalOutput").ap()
    build(nc, A, out)
    r = run_bass_kernel_spmd(nc, [arrays], core_ids=[0])
    return r.results[0]["out_x"]
```

```python
from contextlib import ExitStack

import numpy as np

import concourse.bass as bass
from concourse import mybir

ALU = mybir.AluOpType
ACT = mybir.ActivationFunctionType
AX_X = mybir.AxisListType.X
F32 = mybir.dt.float32
F32R = mybir.dt.float32r
I32 = mybir.dt.int32

P = 128
D = 2048
SEQ = 256
TT = SEQ // P
KT = D // P
NB = 512
NBLK = D // NB
DEPTH = 2
CHUNK = 64
HEADS, NOPE, ROPE, VD = 8, 128, 64, 128
HALF = ROPE // 2
RANK = 512
GH, GDK, GDV, GRANK = 4, 128, 256, 16
W_IN = 4176
CQ, CKV, KR, GQ, GK, GV, LR, GO = 0, 512, 1024, 1088, 1600, 2112, 3136, 3152
GROUPS = 16
NEXP, NGRP, EPG, DEXP = 16, 4, 4, 512
NPAIR = NEXP // 2
CAP = 128
ALPHA = (2.0 * DEPTH) ** 0.25
EPS = 1e-6
BIG = 3.0e38
FAR = 4096.0
C2PI_A, C2PI_B = 6.28125, 0.0019350051879882812
C2PI_C = 2 * np.pi - C2PI_A - C2PI_B
PI_IN = 3.1415925
ROUND = 12582912.0

IN0_FULL = 8
SB_IN0, SB_OUT0 = 0, 9
SB_MOE0 = SB_OUT0 + NBLK
SB_IN1 = SB_MOE0 + 3 * NEXP
SB_OUT1 = SB_IN1 + 8
SB_MOE1 = SB_OUT1 + NBLK
N_ATT_BLOCKS = 2
PAIR_BLOCKS = ((0, 0), (0, 1), (1, 0), (0, 2), (1, 1), (1, 2))
POOL_SLOTS = (0, 2)
T_IN0, T_OUT0, T_IN1, T_OUT1 = range(0, 32, 8)


def land_block(sb):
    return sb + (N_ATT_BLOCKS if sb >= SB_OUT0 else 0)


CONST = {}
_at = 0
for _n, _w in [("ident", P), ("lower", P), ("ones", P), ("suffix", P), ("chunk_of", 2), ("iota0", P), ("iota1", P),
               ("inv_freq", HALF), ("four", NGRP), ("sixteen", NEXP)]:
    CONST[_n] = (_at, _at + _w)
    _at += _w
CW = _at


def constants():
    c = np.zeros((P, CW), np.float32)
    i = np.arange(P)

    def put(name, value):
        a, b = CONST[name]
        c[:, a:b] = value

    put("ident", np.eye(P))
    put("lower", i[:, None] < i[None, :])
    put("ones", 1.0)
    same = (i[:, None] // CHUNK) == (i[None, :] // CHUNK)
    put("suffix", ((i[:, None] > i[None, :]) & same) / 16.0)
    put("chunk_of", ((i[:, None] // CHUNK) == np.arange(2)[None, :]) / 16.0)
    put("iota0", i[None, :])
    put("iota1", CAP + i[None, :])
    put("inv_freq", (np.float32(1) / (10000.0 ** (np.arange(0, ROPE, 2) / ROPE)).astype(np.float32))[None, :])
    put("four", (NGRP - np.arange(NGRP))[None, :])
    put("sixteen", (NEXP - np.arange(NEXP))[None, :])
    return c


FILLS = (
    [("gqT", t, "a") for t in range(TT)] + [("lrT", 0, "a")]
    + [("cqT", t, "v") for t in range(TT)] + [("ckvT", t, "v") for t in range(TT)]
    + [("krT", 0, "a")]
    + [("z", t, "v") for t in range(TT)]
    + [("qr", t, "v") for t in range(TT)]
    + [("qn", i, "a") for i in range(4)]
    + [("suf", t, "a") for t in range(TT)] + [("dec", 0, "a")]
    + [("upd", i, "v") for i in range(8)]
    + [("kn", i, "a") for i in range(4)]
    + [("qrT", i, "a") for i in range(4)]
    + [("ob", i, "v") for i in range(4)]
    + [("s", i, "a") for i in range(6)]
    + [("v", i, "a") for i in range(4)]
    + [("pT", i, "a") for i in range(6)]
    + [("o", i, "v") for i in range(4)]
)
FILL_AT = {(n, i): k for k, (n, i, _) in enumerate(FILLS)}
EMPTIED = {}
for _who in "av":
    for _k, (_n, _i, _w) in enumerate([f for f in FILLS if f[2] == _who]):
        EMPTIED[(_n, _i)] = (_who, _k + 1)


def build(nc, A, out):
    with ExitStack() as ctx:
        def sem(name):
            return ctx.enter_context(nc.semaphore(name))

        at = [0]

        def sb(name, shape, dt=F32, offset=None):
            size = 4 * int(np.prod(shape[1:]))
            if offset is None:
                offset = at[0]
                at[0] += (size + 31) // 32 * 32
            return nc.alloc_sbuf_tensor_at(name, shape, dt, offset=base + offset)

        base = (nc.sbuf_base + 63) // 64 * 64

        w_land = sb("w_land", [P, 4, 4 * NB])
        split_at = at[0]
        w_hi = sb("w_hi", [P, 4, 4 * NB], F32R)
        w_lo = sb("w_lo", [P, 4, 4 * NB], F32R)
        X = sb("X", [P, TT, D])
        t_at = at[0]
        T_hi = sb("T_hi", [P, KT * SEQ], F32R)
        T_lo = sb("T_lo", [P, KT * SEQ], F32R)
        rows_at = at[0]
        rows = sb("rows", [P, 2, D])
        const = sb("const", [P, CW])
        rw = sb("rw", [P, KT, NEXP])
        rbias = sb("rbias", [P, NEXP])
        gains = sb("gains", [P, 2, 4])
        gnorm = sb("gnorm", [P, GDV])
        small = sb("small", [P, 160])
        flag = sb("flag", [P, DEPTH], I32)
        flagf = sb("flagf", [P, DEPTH])
        b_at = at[0]

        xT_hi = T_hi[:, :].rearrange("p (t s) -> p t s", t=KT)
        xT_lo = T_lo[:, :].rearrange("p (t s) -> p t s", t=KT)
        x_hi = T_hi[:, :].rearrange("p (a d) -> p a d", a=TT)
        x_lo = T_lo[:, :].rearrange("p (a d) -> p a d", a=TT)

        def cst(name, n=P):
            a, b = CONST[name]
            return const[0:n, a:b]

        ident = cst("ident")

        H = sb("H", [P, TT, W_IN], offset=b_at)
        r_at = b_at + TT * W_IN * 4
        cosT = sb("cosT", [P, TT, HALF], offset=r_at)
        sinT = sb("sinT", [P, TT, HALF], offset=r_at + 256)
        ropet = sb("ropet", [P, 4, TT, HALF], offset=r_at + 512)
        posi = sb("posi", [P, TT], I32, offset=r_at + 1536)
        posf = sb("posf", [P, TT], offset=r_at + 1568)
        kr_rot = sb("kr_rot", [P, TT, ROPE], offset=r_at + 2624)
        st_at = r_at + 3136
        att = sb("att", [P, 96], offset=st_at)
        o = [split_at]

        def over(name, shape, where=o):
            t = sb(name, shape, offset=where[0])
            where[0] += 4 * int(np.prod(shape[1:]))
            return t

        qnT = over("qnT", [P, HEADS, SEQ])
        knT = over("knT", [P, HEADS, SEQ])
        vv = over("vv", [P, TT, HEADS * VD])
        qrT = over("qrT", [ROPE, HEADS, SEQ])
        sc_at = o[0]
        S0 = over("S0", [P, HEADS, P])
        S1 = over("S1", [P, HEADS, SEQ])
        pT0 = over("pT0", [P, HEADS, P])
        pT1 = over("pT1", [P, HEADS, TT, P])
        states = sb("states", [P, GH, 4, GDV], offset=sc_at)
        qrr = over("qrr", [P, TT, HEADS, ROPE])
        assert o[0] <= t_at - 4 * TT * D
        o2 = [t_at]
        cqT = over("cqT", [P, 4, SEQ], o2)
        ckvT = over("ckvT", [P, 4, SEQ], o2)
        gqT = over("gqT", [P, GH, SEQ], o2)
        lg = over("lg", [P, TT, GH * GDK], o2)
        kdec = over("kdec", [P, TT, GH * GDK], o2)
        la = over("la", [P, TT, GH * GDK], o2)
        krT = over("krT", [ROPE, SEQ], o2)
        lrT = over("lrT", [32, SEQ], o2)
        dec = over("dec", [P, GH, 4], o2)
        rtmp = over("rtmp", [P, 2, HEADS, HALF], o2)
        assert o2[0] <= t_at + 2 * 4 * KT * SEQ
        o3 = [b_at]

        def moe_buf(name, shape, dt=F32):
            t = sb(name, shape, dt, offset=o3[0])
            o3[0] += (4 * int(np.prod(shape[1:])) + 31) // 32 * 32
            return t

        xg_hi = sb("xg_hi", [P, KT, 2 * CAP], F32R, offset=rows_at)
        xg_lo = moe_buf("xg_lo", [P, KT, 2 * CAP], F32R)
        hT_hi = moe_buf("hT_hi", [P, 4, CAP], F32R)
        hT_lo = moe_buf("hT_lo", [P, 4, CAP], F32R)
        hid = moe_buf("hid", [P, DEXP])
        gsil = moe_buf("gsil", [P, DEXP])
        y_hi = moe_buf("y_hi", [P, 2, NB], F32R)
        y_lo = moe_buf("y_lo", [P, 2, NB], F32R)
        place_r = moe_buf("place_r", [P, TT, 2 * CAP], F32R)
        place = moe_buf("place", [P, TT, CAP])
        placeT = moe_buf("placeT", [P, SEQ], F32R)
        route = moe_buf("route", [P, 16, TT, NEXP])
        rank = moe_buf("rank", [P, TT, NEXP])
        comb = moe_buf("comb", [P, TT, NEXP])
        cur = moe_buf("cur", [P, 4, TT])
        rt = sb("rt", [P, 2, 4, SEQ], offset=b_at)
        logitsT = sb("logitsT", [NEXP, SEQ], offset=b_at + 8192)
        o4 = [b_at]
        UV = over("UV", [P, TT, 2 * D], o4)
        U, V = UV[:, :, 0:D], UV[:, :, D:2 * D]
        ws = over("ws", [P, GROUPS, P], o4)
        bs = over("bs", [GROUPS, P], o4)
        bsT = over("bsT", [P, GROUPS], o4)
        end = max(st_at + 400, o3[0], o4[0])
        assert base + end <= nc.sbuf_usable_end, (base + end, nc.sbuf_usable_end)

        stats = small[:, 0:TT * 4 * 6].rearrange("p (a n s) -> p a n s", a=TT, n=4)
        meanvar = small[:, 48:52].rearrange("p (a s) -> p a s", a=TT)
        inv_var = small[:, 52:54]
        rstd = small[:, 54:56]
        shift = small[:, 56:58]

        bank = [ctx.enter_context(nc.psum_tensor(f"bank{i}", [P, NB], F32)) for i in range(8)]

        ident_in, const_in, rows_in, ws_in = sem("ident_in"), sem("const_in"), sem("rows_in"), sem("ws_in")
        x_in = [sem(f"x_in{q}") for q in range(4)]
        out_stored = sem("out_stored")
        t_filled, t_high, t_low = sem("t_filled"), sem("t_high"), sem("t_low")
        gemm_out_a, gemm_out_v = sem("gemm_out_a"), sem("gemm_out_v")
        rows_used = sem("rows_used")
        ln_recip, ln_root, ln_shift, ln_scaled, x_ready = (sem(n) for n in ("ln_recip", "ln_root", "ln_shift",
                                                                              "ln_scaled", "x_ready"))
        r_filled, r_out, logits_out = sem("r_filled"), sem("r_out"), sem("logits_out")
        att_filled, att_out_a, att_out_v = sem("att_filled"), sem("att_out_a"), sem("att_out_v")
        bias_in = sem("bias_in")
        trig_ready, trig_done = sem("trig_ready"), sem("trig_done")
        rms_sq, rms_rec, rms_root, c_normed, kr_rotated, ones_set = (sem(n) for n in (
            "rms_sq", "rms_rec", "rms_root", "c_normed", "kr_rotated", "ones_set"))
        z_soft, logg_ready, kdec_ready, go_silu, ob_sq, ob_rec, ob_root = (sem(n) for n in (
            "z_soft", "logg_ready", "kdec_ready", "go_silu", "ob_sq", "ob_rec", "ob_root"))
        qr_rotated, s_shifted, p_ready = (sem(n) for n in ("qr_rotated", "s_shifted", "p_ready"))
        x_high, x_low = sem("x_high"), sem("x_low")
        logits_done, sigm_done, sel_ready, rank_done, rank_ready, flag_ready, x_scaled = (sem(n) for n in (
            "logits_done", "sigm_done", "sel_ready", "rank_done", "rank_ready", "flag_ready", "x_scaled"))
        sgu_filled, sgu_out, wsT_copied, wsT_ready, v_ready, moe_over = (sem(n) for n in (
            "sgu_filled", "sgu_out", "wsT_copied", "wsT_ready", "v_ready", "moe_over"))
        chain_a, chain_v = sem("chain_a"), sem("chain_v")

        class Stream:

            def __init__(self, tag):
                def s(name):
                    return sem(tag + name)

                self.landed = [s(f"landed{j}") for j in range(4)]
                self.lo_done = [s(f"lo_done{j}") for j in range(4)]
                self.hi_done, self.used = s("hi_done"), s("used")
                self.xg_fill_h, self.xg_fill_l = s("xg_fill_h"), s("xg_fill_l")
                self.xg_out_h, self.xg_out_l = s("xg_out_h"), s("xg_out_l")
                self.silu_done, self.h_done, self.hT_fill = s("silu_done"), s("h_done"), s("hT_fill")
                self.hT_hi_done, self.hT_lo_done = s("hT_hi_done"), s("hT_lo_done")
                self.cur_ready, self.cur_seen, self.cur_v = s("cur_ready"), s("cur_seen"), s("cur_v")
                self.place_ready, self.place_r_ready = s("place_ready"), s("place_r_ready")
                self.pt_fill, self.pt_done = s("pt_fill"), s("pt_done")
                self.y_hi_done, self.y_lo_done, self.scat_fill = s("y_hi_done"), s("y_lo_done"), s("scat_fill")
                self.acc0_done, self.acc_done = s("acc0_done"), s("acc_done")
                if tag:
                    self.stats_done = s("stats_done")

        main = Stream("")
        overflow = [Stream(f"over{layer}_") for layer in range(DEPTH)]
        landed = main.landed

        def ge(eng, s, value):
            if not (isinstance(value, int) and value <= 0):
                eng.wait_ge(s, value)

        class Chain:

            def __init__(self, eng, s):
                self.eng, self.s, self.n = eng, s, 0

            def __call__(self, ins):
                self.n += 1
                ins.then_inc(self.s, 1)

            def wait(self):
                self.eng.wait_ge(self.s, self.n)

        w_in0 = A["ev_w_in"][0].rearrange("(t p) n -> p t n", p=P)
        w_in1 = A["od_w_in"][0].rearrange("(t p) n -> p t n", p=P)
        w_out1 = A["od_w_out"][0].rearrange("(t p) n -> p t n", p=P)
        w_out0 = A["ev_w_out"][0].rearrange("(h t p) n -> h p t n", h=2, p=P)
        w_uq = A["ev_w_uq"][0].rearrange("(p c) h d -> p c h d", c=4)
        w_ukv = A["ev_w_ukv"][0].rearrange("(p c) h d -> p c h d", c=4)
        out_v = out.rearrange("b (a p) d -> p (b a) d", p=P)
        x_v = A["x"].rearrange("b (a p) d -> p (b a) d", p=P)
        pos_v = A["positions"].rearrange("b (a p) -> p (b a)", p=P)

        def land(j, n=NB):
            return w_land[:, j, 0:4 * n].rearrange("p (c n) -> p c n", c=4)

        def hi(j, n=NB):
            return w_hi[:, j, 0:4 * n].rearrange("p (c n) -> p c n", c=4)

        def lo(j, n=NB):
            return w_lo[:, j, 0:4 * n].rearrange("p (c n) -> p c n", c=4)

        def moe_src(layer, e, part, j):
            if part < 2:
                w = A[("moe_w_gate", "moe_w_up")[part]][layer, bass.ds(e, 1)]
                return w.rearrange("o (p t) n -> (o p) t n", t=KT)[:, 4 * j:4 * j + 4, :]
            w = A["moe_w_down"][layer, bass.ds(e, 1)]
            return w.rearrange("o (p t) n -> (o p) t n", t=4)[:, :, j * NB:(j + 1) * NB]

        def over_pairs(eng, body):
            body(0, True, False)
            with eng.Fori(1, NPAIR - 1) as p:
                body(p, False, False)
            body(NPAIR - 1, False, True)

        block = ctx.enter_context(nc.Block())

        @block.sync
        def _(sp):
            sp.dma_start(const[:], A["const"]).then_inc(ident_in, 16)

            def load(lb, j, src, s=main, n=NB):
                sp.dma_start(land(j, n), src).then_inc(s.landed[j], 16)

            for j in range(4):
                sp.dma_start(X[:, :, j * NB:(j + 1) * NB], x_v[:, :, j * NB:(j + 1) * NB]).then_inc(x_in[j], 16)
                load(0, j, w_in0[:, 4 * j:4 * j + 4, 0:NB])
            with sp.Fori(1, IN0_FULL) as b:
                for j in range(4):
                    sp.wait_ge(main.lo_done[j], b)
                    load(b, j, w_in0[:, 4 * j:4 * j + 4, bass.ds(b * NB, NB)])
            tail = W_IN - IN0_FULL * NB
            for j in range(4):
                sp.wait_ge(main.lo_done[j], IN0_FULL)
                load(IN0_FULL, j, w_in0[:, 4 * j:4 * j + 4, IN0_FULL * NB:W_IN], n=tail)
            att_units = (
                [None, w_uq[:, :, :, NOPE:NOPE + ROPE], w_uq[:, :, 0:4, 0:NOPE], w_uq[:, :, 4:8, 0:NOPE]],
                [w_ukv[:, :, 0:4, 0:NOPE], w_ukv[:, :, 4:8, 0:NOPE], w_ukv[:, :, 0:4, NOPE:], w_ukv[:, :, 4:8, NOPE:]],
            )
            for b in range(2):
                for j in range(4):
                    if b == 0:
                        sp.wait_ge(main.lo_done[j], IN0_FULL + 1)
                    else:
                        sp.wait_ge(att_filled, FILL_AT[(("z", 1), ("qr", 1), ("qn", 1), ("qn", 3))[j]] + 1)
                    if b == 0 and j == 0:
                        sp.dma_start(w_land[0:GRANK, 0, 0:NB], A["ev_w_gk2"][0]).then_inc(landed[0], 16)
                        sp.dma_start(w_land[GRANK:GRANK + 1, 0, 0:NB], A["ev_b_gk2"]).then_inc(bias_in, 16)
                        continue
                    src = att_units[b][j]
                    heads = src.shape[2]
                    sp.dma_start(w_land[:, j, :].rearrange("p (c h d) -> p c h d", c=4, h=heads), src) \
                        .then_inc(landed[j], 16)
            for b in range(NBLK):
                for j in range(4):
                    if b == 0:
                        sp.wait_ge(att_filled, FILL_AT[(("kn", 1), ("kn", 3), ("v", 1), ("v", 3))[j]] + 1)
                    else:
                        sp.wait_ge(main.lo_done[j], SB_OUT0 + b)
                    load(0, j, w_out0[1 - j // 2, :, 4 * (j % 2):4 * (j % 2) + 4, b * NB:(b + 1) * NB])

            def experts(layer, s, sb0):
                def body(p, first, last):
                    for b, (k, part) in enumerate(PAIR_BLOCKS):
                        for j in range(4):
                            if not (first and b == 0 and sb0 == 0):
                                sp.wait_ge(s.lo_done[j], sb0 + 6 * p + b)
                            load(0, j, moe_src(layer, 2 * p + k, part, j), s)
                over_pairs(sp, body)

            def overflow_pass(layer):
                sp.wait_ge(flag_ready, layer + 1)
                many = sp.value_load(flag[0:1, layer:layer + 1])
                with sp.If(many > CAP):
                    for j in range(4):
                        sp.wait_ge(main.lo_done[j], (SB_MOE0, SB_MOE1)[layer] + 3 * NEXP)
                    experts(layer, overflow[layer], 0)
                    for j in range(4):
                        sp.wait_ge(overflow[layer].lo_done[j], 3 * NEXP)

            experts(0, main, SB_MOE0)
            overflow_pass(0)
            for sb1, first in ((SB_IN1, NBLK), (SB_IN1 + NBLK, 0)):
                with sp.Fori(0, NBLK) as b:
                    for j in range(4):
                        sp.wait_ge(main.lo_done[j], sb1 + b)
                        load(0, j, w_in1[:, 4 * j:4 * j + 4, bass.ds((first + b) * NB, NB)])
            for b in range(NBLK):
                for j in range(4):
                    sp.wait_ge(main.lo_done[j], SB_OUT1 + b)
                    load(0, j, w_out1[:, 4 * j:4 * j + 4, b * NB:(b + 1) * NB])
            experts(1, main, SB_MOE1)
            overflow_pass(1)
            for k in range(TT * NBLK):
                n, a = k // TT, k % TT
                sp.wait_ge(x_ready, 3 * TT * NBLK + k + 1)
                sp.dma_start(out_v[:, a, n * NB:(n + 1) * NB], X[:, a, n * NB:(n + 1) * NB]).then_inc(out_stored, 16)
            sp.wait_ge(out_stored, 16 * TT * NBLK)

        @block.gpsimd
        def _(pool):
            for dst, src in ((rw[:], A["router_w"].rearrange("(t p) e -> p t e", p=P)),
                             (rbias[:], A["router_b"].rearrange("(o e) -> o e", o=1).partition_broadcast(P)),
                             (gains[:, 0, :], A["ev_q_norm"][0].rearrange("(p t) -> p t", t=4)),
                             (gains[:, 1, :], A["ev_kv_norm"][0].rearrange("(p t) -> p t", t=4)),
                             (gnorm[:], A["ev_gla_norm"].partition_broadcast(P)),
                             (posi[:], pos_v)):
                pool.dma_start(dst, src, allow_slow_non_contiguous=True).then_inc(const_in, 16)

            def load_rows(g, b, n):
                if n:
                    pool.wait_ge(rows_used, n)
                pool.dma_start(rows[:, 0, :], g.partition_broadcast(P)).then_inc(rows_in, 16)
                pool.dma_start(rows[:, 1, :], b.partition_broadcast(P)).then_inc(rows_in, 16)

            def low_parts(sb, s=main, js=range(4)):
                for j in js:
                    pool.wait_ge(s.hi_done, 4 * sb + j + 1)
                    pool.tensor_tensor(w_lo[:, j, :], w_land[:, j, :], w_hi[:, j, :], ALU.subtract) \
                        .then_inc(s.lo_done[j], 1)

            def experts(layer, s, sb0, p0, iota):
                def one_hot(dst, k, col):
                    for a in range(TT):
                        ins = pool.tensor_scalar(dst[:, a, k * CAP:(k + 1) * CAP], cst(iota), cur[:, col, a:a + 1],
                                                 None, ALU.is_equal)
                    return ins

                def ranks_read(count):
                    pool.wait_ge(s.cur_ready, count)
                    pool.sem_inc(s.cur_seen, 1)

                def one(e, count):
                    pool.tensor_copy(cur[:, 0, :], rank[:, :, bass.ds(e, 1)].rearrange("p a o -> p (a o)")) \
                        .then_inc(s.cur_ready, 1)
                    ranks_read(count)
                    one_hot(place, 0, 0).then_inc(s.place_ready, 1)

                def pair(p, count):
                    pool.tensor_copy(cur[:, 1:3, :], rank[:, :, bass.ds(2 * p, 2)].rearrange("p a o -> p o a")) \
                        .then_inc(s.cur_ready, 1)
                    ranks_read(count)
                    one_hot(place_r, 0, 1)
                    one_hot(place_r, 1, 2).then_inc(s.place_r_ready, 1)

                def body(p, first, last):
                    C, E = (0 if s is main else 1) + (3 * NPAIR - 1) * (p0 // NPAIR) + 3 * p, 2 * (p0 + p)
                    ge(pool, s.pt_fill, E)
                    one(2 * p, C + 1)
                    if not last:
                        pool.wait_ge(s.xg_fill_l, 8 * (p0 + p + 1))
                        pair(p + 1, C + 2)
                    pool.wait_ge(s.pt_fill, E + 1)
                    one(2 * p + 1, C + (2 if last else 3))
                    for b in (4,) if last else (4, 6):
                        low_parts(sb0 + 6 * p + b, s, POOL_SLOTS)

                if s is not main:
                    pair(0, 1)
                else:
                    low_parts(sb0, js=[2, 3])
                    pool.wait_ge(r_filled, 8 * (layer + 1))
                    pool.wait_ge(x_low, 8 * (layer + 1))
                    for a in range(TT):
                        ins = pool.tensor_scalar(X[:, a, :], X[:, a, :], ALPHA, None, ALU.mult)
                    ins.then_inc(x_scaled, 1)
                over_pairs(pool, body)

            def moe(layer):
                low_parts((SB_MOE0, SB_MOE1)[layer], js=[0, 1])
                pool.wait_ge(rank_ready, layer + 1)
                pool.wait_ge(flag_ready, layer + 1)
                experts(layer, main, (SB_MOE0, SB_MOE1)[layer], layer * NPAIR, "iota0")
                many = pool.value_load(flag[0:1, layer:layer + 1])
                with pool.If(many > CAP):
                    pool.wait_ge(main.scat_fill, 4 * NEXP * (layer + 1))
                    experts(layer, overflow[layer], 0, 0, "iota1")
                    pool.wait_ge(overflow[layer].h_done, NEXP)
                pool.wait_ge(main.h_done, NEXP * (layer + 1))
                load_rows(A["ln_ffn_g"][layer:layer + 1], A["ln_ffn_b"][layer:layer + 1], (1, 4)[layer])

            load_rows(A["ln_mix_g"][0:1], A["ln_mix_b"][0:1], 0)
            pool.wait_ge(ident_in, 16)
            moe(0)
            low_parts(SB_IN1)
            load_rows(A["od_sgu_ln_g"], A["od_sgu_ln_b"], 2)
            pool.wait_ge(moe_over, 1)
            pool.dma_start(ws[:], A["od_w_s"][0].rearrange("g i j -> i g j")).then_inc(ws_in, 16)
            pool.dma_start(bs[:], A["od_b_s"][0]).then_inc(ws_in, 16)
            load_rows(A["ln_mix_g"][1:2], A["ln_mix_b"][1:2], 3)
            moe(1)

        @block.tensor
        def _(pe):
            def three(dst, hi_l, lo_l, hi_r, lo_r, start, stop):
                pe.matmul(dst, hi_l, hi_r, start=start, stop=False)
                pe.matmul(dst, hi_l, lo_r, start=False, stop=False)
                return pe.matmul(dst, lo_l, hi_r, start=False, stop=stop)

            def transposes(t0, q, src, ready):
                for a in range(TT):
                    g = 2 * q + a
                    ready(q, a)
                    if g >= 4:
                        pe.wait_ge(t_low, t0 + g - 3)
                    for c in range(4):
                        ins = pe.transpose(bank[4 + (g + 2) % 4][:, c * P:(c + 1) * P], src(a, 4 * q + c), ident)
                    ins.then_inc(t_filled, 1)

            def gemm_unit(sb, pair, j, n=NB):
                pe.wait_ge(main.lo_done[j], sb + 1)
                for a in range(TT):
                    for c in range(4):
                        t = 4 * j + c
                        ins = three(bank[2 * pair + a][:, 0:n], xT_hi[:, t, a * P:(a + 1) * P],
                                    xT_lo[:, t, a * P:(a + 1) * P], hi(j, n)[:, c, :], lo(j, n)[:, c, :],
                                    t == 0, t == KT - 1)
                ins.then_inc(main.used, 1)

            def gemm_block(sb, pair, n=NB):
                for j in range(4):
                    gemm_unit(sb, pair, j, n)

            def first_block(sb, t0, src, ready, after_first=lambda: None):
                transposes(t0, 0, src, ready)
                after_first()
                transposes(t0, 1, src, ready)
                for j in range(4):
                    pe.wait_ge(t_low, t0 + 2 * j + 2)
                    gemm_unit(sb, 0, j)
                    if j < 2:
                        transposes(t0, j + 2, src, ready)

            pe.wait_ge(ident_in, 16)
            first_block(0, T_IN0, lambda a, t: X[:, a, t * P:(t + 1) * P], lambda q, a: pe.wait_ge(x_in[q], 16))
            gemm_block(1, 1)
            with pe.Fori(1, IN0_FULL // 2) as i:
                for p in range(2):
                    pe.wait_ge(gemm_out_a, 2 * i + p - 1)
                    pe.wait_ge(gemm_out_v, 2 * i + p - 1)
                    gemm_block(2 * i + p, p)
            pe.wait_ge(gemm_out_a, IN0_FULL - 1)
            pe.wait_ge(gemm_out_v, IN0_FULL - 1)
            gemm_block(IN0_FULL, 0, W_IN - IN0_FULL * NB)
            pe.wait_ge(gemm_out_a, IN0_FULL + 1)
            pe.wait_ge(gemm_out_v, IN0_FULL + 1)

            def begin(name, i=0):
                k = FILL_AT[(name, i)]
                if k >= 8:
                    emptied(*FILLS[k - 8][:2])
                return bank[k % 8]

            def emptied(name, i=0):
                who, n = EMPTIED[(name, i)]
                pe.wait_ge(att_out_a if who == "a" else att_out_v, n)

            def end(ins):
                ins.then_inc(att_filled, 1)

            for a in range(TT):
                b = begin("gqT", a)
                for h in range(GH):
                    ins = pe.transpose(b[:, h * P:(h + 1) * P], H[:, a, GQ + h * GDK:GQ + (h + 1) * GDK], ident)
                end(ins)
            b = begin("lrT")
            for a in range(TT):
                ins = pe.transpose(b[0:GRANK, a * P:(a + 1) * P], H[:, a, LR:LR + GRANK], ident)
            end(ins)
            for w, (name, c0) in enumerate((("cqT", CQ), ("ckvT", CKV))):
                for a in range(TT):
                    b = begin(name, a)
                    pe.wait_ge(c_normed, 2 * w + a + 1)
                    for t in range(4):
                        ins = pe.transpose(b[:, t * P:(t + 1) * P], H[:, a, c0 + t:c0 + RANK:4], ident)
                    end(ins)
            b = begin("krT")
            pe.wait_ge(kr_rotated, 1)
            for a in range(TT):
                ins = pe.transpose(b[0:ROPE, a * P:(a + 1) * P], kr_rot[:, a, :], ident)
            end(ins)
            pe.wait_ge(landed[0], 16 * (IN0_FULL + 2))
            pe.wait_ge(bias_in, 16)
            emptied("lrT")
            for a in range(TT):
                b = begin("z", a)
                ins = pe.matmul(b[:], lrT[0:GRANK + 1, a * P:(a + 1) * P], w_land[0:GRANK + 1, 0, 0:NB],
                                start=True, stop=True)
                end(ins)
            emptied("cqT", 1)
            pe.wait_ge(landed[1], 16 * (IN0_FULL + 2))
            for a in range(TT):
                b = begin("qr", a)
                for c in range(4):
                    ins = pe.matmul(b[:], cqT[:, c, a * P:(a + 1) * P], land(1)[:, c, :], start=c == 0, stop=c == 3)
                end(ins)

            def per_head(name, i, slot, rhs):
                b = begin(name, i)
                for k in range(2):
                    h = (2 * i + k) % 4
                    for c in range(4):
                        ins = pe.matmul(b[:, k * SEQ:(k + 1) * SEQ], land(slot)[:, c, h * P:(h + 1) * P], rhs[:, c, :],
                                        start=c == 0, stop=c == 3)
                end(ins)

            for i in range(4):
                if i % 2 == 0:
                    pe.wait_ge(landed[2 + i // 2], 16 * (IN0_FULL + 2))
                per_head("qn", i, 2 + i // 2, cqT)
            for a in range(TT):
                b = begin("suf", a)
                pe.wait_ge(logg_ready, a + 1)
                end(pe.matmul(b[:], cst("suffix"), lg[:, a, :], start=True, stop=True))
            b = begin("dec")
            for a in range(TT):
                for h in range(GH):
                    ins = pe.matmul(b[:, 2 * (TT * h + a):2 * (TT * h + a) + 2], lg[:, a, h * GDK:(h + 1) * GDK],
                                    cst("chunk_of"), start=True, stop=True)
            end(ins)
            pe.wait_ge(kdec_ready, TT)
            for i in range(8):
                b = begin("upd", i)
                for k in range(2):
                    c, h = (2 * i + k) // GH, (2 * i + k) % GH
                    r = slice(CHUNK * (c % 2), CHUNK * (c % 2) + CHUNK)
                    ins = pe.matmul(b[:, k * GDV:(k + 1) * GDV], kdec[r, c // 2, h * GDK:(h + 1) * GDK],
                                    H[r, c // 2, GV + h * GDV:GV + (h + 1) * GDV], start=True, stop=True)
                end(ins)
            emptied("ckvT", 1)
            for i in range(4):
                if i % 2 == 0:
                    pe.wait_ge(landed[i // 2], 16 * (IN0_FULL + 3))
                per_head("kn", i, i // 2, ckvT)
            for i in range(4):
                a, q = i // 2, i % 2
                b = begin("qrT", i)
                pe.wait_ge(qr_rotated, a + 1)
                for k in range(4):
                    ins = pe.transpose(b[0:ROPE, k * P:(k + 1) * P], qrr[:, a, 4 * q + k, :], ident)
                end(ins)
            emptied("upd", 7)
            emptied("gqT", 1)
            for i in range(4):
                a, q = i // 2, i % 2
                b = begin("ob", i)
                for k in range(2):
                    h = 2 * q + k
                    for cc in range(2):
                        s = slice(a * P + cc * CHUNK, a * P + (cc + 1) * CHUNK)
                        ins = pe.matmul(b[cc * CHUNK:(cc + 1) * CHUNK, k * GDV:(k + 1) * GDV], gqT[:, h, s],
                                        states[:, h, 2 * a + cc, :], start=True, stop=True)
                end(ins)
            emptied("kn", 3)
            emptied("qrT", 3)
            for i in range(6):
                a = 0 if i < 2 else 1
                keys = P * (a + 1)
                per = NB // keys
                h0 = i * 4 if a == 0 else (i - 2) * 2
                b = begin("s", i)
                for k in range(per):
                    h = h0 + k
                    dst = b[:, k * keys:(k + 1) * keys]
                    pe.matmul(dst, qnT[:, h, a * P:(a + 1) * P], knT[:, h, 0:keys], start=True, stop=False)
                    ins = pe.matmul(dst, qrT[:, h, a * P:(a + 1) * P], krT[:, 0:keys], start=False, stop=True)
                end(ins)
            for i in range(4):
                half, a = i // 2, i % 2
                if a == 0:
                    pe.wait_ge(landed[2 + half], 16 * (IN0_FULL + 3))
                b = begin("v", i)
                for c in range(4):
                    ins = pe.matmul(b[:], ckvT[:, c, a * P:(a + 1) * P], land(2 + half)[:, c, :],
                                    start=c == 0, stop=c == 3)
                end(ins)
            for i in range(6):
                b = begin("pT", i)
                pe.wait_ge(p_ready, 1 if i < 2 else 2)
                for k in range(4):
                    if i < 2:
                        src = S0[:, 4 * i + k, :]
                    else:
                        m = 4 * (i - 2) + k
                        src = S1[:, m // 2, (m % 2) * P:(m % 2 + 1) * P]
                    ins = pe.transpose(b[:, k * P:(k + 1) * P], src, ident)
                end(ins)
            emptied("pT", 5)
            emptied("v", 3)
            for i in range(4):
                a, q = i // 2, i % 2
                b = begin("o", i)
                for k in range(4):
                    h = 4 * q + k
                    for kb in range(a + 1):
                        pt = pT0[:, h, :] if a == 0 else pT1[:, h, kb, :]
                        ins = pe.matmul(b[:, k * P:(k + 1) * P], pt, vv[:, kb, h * VD:(h + 1) * VD],
                                        start=kb == 0, stop=kb == a)
                end(ins)
            def out_projection(sb0, ev0, t0, src, ready, after_first=lambda: None):
                first_block(sb0, t0, src, ready, after_first)
                for b in range(1, NBLK):
                    if b >= 2:
                        pe.wait_ge(gemm_out_v, ev0 + 2 * (b - 1))
                    gemm_block(sb0 + b, b % 2)

            out_projection(SB_OUT0, IN0_FULL + 1, T_OUT0,
                           lambda a, t: H[:, a, (GV, 0)[t // 8] + t % 8 * P:(GV, 0)[t // 8] + t % 8 * P + P],
                           lambda q, a: emptied("o", 3 if q >= 2 else 0))

            def route_tokens(layer):
                if layer == 0:
                    pe.wait_ge(const_in, 16 * 6)

                def logits(q):
                    pe.wait_ge(r_out, 8 * layer + 2 * q + 2)
                    for c in range(4):
                        t = 4 * q + c
                        ins = pe.matmul(bank[7][0:NEXP, 0:SEQ], rw[:, t, :], rt[:, q % 2, c, :],
                                        start=t == 0, stop=t == KT - 1)
                    return ins

                for g in range(8):
                    q, a = g // 2, g % 2
                    pe.wait_ge(x_ready, 16 * layer + g + 1)
                    if g >= 2:
                        pe.wait_ge(r_out, 8 * layer + g - 1)
                    for c in range(4):
                        t = 4 * q + c
                        ins = pe.transpose(bank[4 + g % 2][:, c * P:(c + 1) * P], X[:, a, t * P:(t + 1) * P], ident)
                    ins.then_inc(r_filled, 1)
                    if g >= 3 and a:
                        logits(q - 1)
                logits(3).then_inc(logits_done, 1)
                pe.wait_ge(logits_out, layer + 1)
                for a in range(TT):
                    ins = pe.transpose(bank[6][:, a * NEXP:(a + 1) * NEXP], logitsT[:, a * P:(a + 1) * P],
                                       const[0:NEXP, 0:NEXP])
                ins.then_inc(logits_done, 1)
                pe.wait_ge(sel_ready, layer + 1)
                sel = route[:, 15]
                for a in range(TT):
                    dst = bank[6][:, 64 + 32 * a:64 + 32 * a + NEXP]
                    if a:
                        pe.matmul(dst, cst("ones"), sel[:, 0, :], start=True, stop=False)
                    pe.matmul(dst, cst("lower"), sel[:, a, :], start=a == 0, stop=True)
                for a in range(TT):
                    ins = pe.matmul(bank[6][:, 128:128 + NEXP], cst("ones"), sel[:, a, :], start=a == 0, stop=a == 1)
                ins.then_inc(rank_done, 1)

            def gather(s, pair, groups):
                for q, part in [(q, part) for q in groups for part in range(2)]:
                    src = (x_hi, x_lo)[part]
                    dst = bank[4 + 2 * (q % 2) + part]
                    ge(pe, (s.xg_out_h, s.xg_out_l)[part], 8 * pair + q - 1)
                    for c in range(2):
                        t = 2 * q + c
                        for a in range(TT):
                            ins = pe.matmul(dst[:, c * 2 * CAP:(c + 1) * 2 * CAP], src[:, a, t:D:KT],
                                            place_r[:, a, :], start=a == 0, stop=a == TT - 1)
                    ins.then_inc((s.xg_fill_h, s.xg_fill_l)[part], 1)

            def scatter(s, m, half, gathered):
                pe.wait_ge(s.y_lo_done, m + 1)
                ge(pe, s.acc_done, m)
                ge(pe, s.xg_out_h, gathered)
                ge(pe, s.xg_out_l, gathered)
                for a in range(TT):
                    pe.matmul(bank[6 + a][:], placeT[:, a * P:(a + 1) * P], y_hi[:, half, :], start=True, stop=False)
                    ins = pe.matmul(bank[6 + a][:], placeT[:, a * P:(a + 1) * P], y_lo[:, half, :],
                                    start=False, stop=True)
                ins.then_inc(s.scat_fill, 1)

            def experts(layer, s, sb0, p0):
                pe.wait_ge(s.place_r_ready, p0 + 1)
                if s is main:
                    pe.wait_ge(flag_ready, p0 // NPAIR + 1)
                gather(s, p0, range(8))

                def body(p, first, last):
                    pair, B = p0 + p, sb0 + 6 * p

                    def up_gate(b, k, part, js):
                        for j in js:
                            pe.wait_ge(s.lo_done[j], B + b + 1)
                            for c in range(4):
                                t = 4 * j + c
                                ins = three(bank[part][:], xg_hi[:, t, k * CAP:(k + 1) * CAP],
                                            xg_lo[:, t, k * CAP:(k + 1) * CAP], hi(j)[:, c, :], lo(j)[:, c, :],
                                            t == 0, t == KT - 1)
                            ins.then_inc(s.used, 1)

                    def slots(E):
                        pe.wait_ge(s.place_ready, E + 1)
                        for a in range(TT):
                            ins = pe.transpose(bank[2][:, a * P:(a + 1) * P], place[:, a, :], ident)
                        ins.then_inc(s.pt_fill, 1)

                    def hidden(E):
                        pe.wait_ge(s.h_done, E + 1)
                        for c in range(4):
                            ins = pe.transpose(bank[3][:, c * P:(c + 1) * P], hid[:, c:DEXP:4], ident)
                        ins.then_inc(s.hT_fill, 1)

                    def down(b, E, gathered):
                        for n in range(4):
                            pe.wait_ge(s.lo_done[n], B + b + 1)
                            if n == 0:
                                pe.wait_ge(s.hT_lo_done, E + 1)
                                pe.wait_ge(s.pt_done, E + 1)
                            if n >= 2:
                                pe.wait_ge(s.y_lo_done, 4 * E + n - 1)
                            for c in range(4):
                                ins = three(bank[2 + n % 2][:], hT_hi[:, c, :], hT_lo[:, c, :], hi(n)[:, c, :],
                                            lo(n)[:, c, :], c == 0, c == 3)
                            ins.then_inc(s.used, 1)
                            if n:
                                scatter(s, 4 * E + n - 1, (n - 1) % 2, gathered)

                    E0, E1 = 2 * pair, 2 * pair + 1
                    ge(pe, s.silu_done, E0)
                    pe.wait_ge(s.xg_out_h, 8 * (pair + 1))
                    pe.wait_ge(s.xg_out_l, 8 * (pair + 1))
                    up_gate(0, 0, 0, [0])
                    if not first:
                        scatter(s, 4 * E0 - 1, 1, 8 * (pair + 1))
                    up_gate(0, 0, 0, [1, 2, 3])
                    ge(pe, s.h_done, E0)
                    up_gate(1, 0, 1, range(4))
                    pe.wait_ge(s.silu_done, E0 + 1)
                    up_gate(2, 1, 0, [0, 1])
                    slots(E0)
                    hidden(E0)
                    up_gate(2, 1, 0, [2, 3])
                    down(3, E0, 8 * (pair + 1))
                    up_gate(4, 1, 1, [0])
                    scatter(s, 4 * E0 + 3, 1, 8 * (pair + 1))
                    up_gate(4, 1, 1, [1])
                    if not last:
                        pe.wait_ge(s.place_r_ready, pair + 2)
                        pe.wait_ge(s.acc_done, 4 * E1)
                        gather(s, pair + 1, [0, 1])
                    up_gate(4, 1, 1, [2])
                    if not last:
                        gather(s, pair + 1, [2, 3])
                    up_gate(4, 1, 1, [3])
                    slots(E1)
                    if not last:
                        gather(s, pair + 1, [4, 5])
                    hidden(E1)
                    if not last:
                        gather(s, pair + 1, [6, 7])
                    down(5, E1, 8 * (pair + (1 if last else 2)))
                    if last:
                        scatter(s, 4 * E1 + 3, 1, 8 * (pair + 1))
                over_pairs(pe, body)

            def moe(layer):
                route_tokens(layer)
                pe.wait_ge(x_low, 8 * (layer + 1))
                experts(layer, main, (SB_MOE0, SB_MOE1)[layer], layer * NPAIR)
                pe.wait_ge(flag_ready, layer + 1)
                many = pe.value_load(flag[0:1, layer:layer + 1])
                with pe.If(many > CAP):
                    pe.wait_ge(main.acc_done, 4 * NEXP * (layer + 1))
                    experts(layer, overflow[layer], 0, 0)

            moe(0)
            first_block(SB_IN1, T_IN1, lambda a, t: X[:, a, t * P:(t + 1) * P],
                        lambda q, a: pe.wait_ge(x_ready, 8 + 2 * q + a + 1))
            gemm_block(SB_IN1 + 1, 1)
            pe.wait_ge(ws_in, 32)
            pe.wait_ge(t_low, T_IN1 + 8)
            for i in range(4):
                for k in range(4):
                    ins = pe.transpose(bank[4 + i][:, k * P:(k + 1) * P], ws[:, 4 * i + k, :], ident)
                ins.then_inc(sgu_filled, 1)

            def gate(n):
                pe.wait_ge(v_ready, 2 * n + 2)
                for i in (2 * n, 2 * n + 1):
                    ge(pe, sgu_out, i - 1)
                    for k in range(2):
                        g = 2 * i + k
                        ins = pe.matmul(bank[4 + i % 2][:, k * 2 * P:(k + 1) * 2 * P].rearrange("p (a c) -> p a c", a=TT),
                                        ws[:, g, :], V[:, :, g * P:(g + 1) * P], start=True, stop=True)
                    ins.then_inc(sgu_filled, 1)

            for b in range(2, 8):
                pe.wait_ge(gemm_out_a, IN0_FULL + 1 + 2 * (b - 1))
                gemm_block(SB_IN1 + b, b % 2)
                if b == 2:
                    pe.wait_ge(wsT_copied, 1)
                    pe.transpose(bank[4][:, 0:GROUPS], bs[:, :], const[0:GROUPS, 0:GROUPS]).then_inc(sgu_filled, 1)
                if b == 5:
                    pe.wait_ge(wsT_ready, 1)
                if b >= 5:
                    gate(b - 5)

            def last_gate():
                gate(3)
                pe.wait_ge(gemm_out_a, IN0_FULL + 1 + 16)

            out_projection(SB_OUT1, IN0_FULL + 1 + 8, T_OUT1, lambda a, t: U[:, a, t * P:(t + 1) * P],
                           lambda q, a: pe.wait_ge(sgu_out, 8 if q else 2), last_gate)
            moe(1)

        @block.scalar
        def _(act):
            chain = Chain(act, chain_a)

            def split(sb, lb, s=main, n=NB, js=range(4)):
                for j in js:
                    act.wait_ge(s.landed[j], 16 * (lb + 1))
                    ge(act, s.used, 4 * (sb - 1) + j + 1)
                    act.copy(w_hi[:, j, 0:4 * n], w_land[:, j, 0:4 * n]).then_inc(s.hi_done, 1)

            def transposed(t0, g):
                q, a = g // 2, g % 2
                act.wait_ge(t_filled, t0 + g + 1)
                act.copy(xT_hi[:, 4 * q:4 * q + 4, a * P:(a + 1) * P],
                         bank[4 + (g + 2) % 4][:].rearrange("p (c s) -> p c s", c=4)).then_inc(t_high, 1)

            def first_block(sb, lb, t0, done=0):
                for j in range(2):
                    transposed(t0, 2 * j)
                    transposed(t0, 2 * j + 1)
                    if j >= done:
                        split(sb, lb, js=[j])
                split(sb, lb, js=[2, 3])
                for g in range(4, 8):
                    transposed(t0, g)

            def layer_norm(k, after=lambda m: None):
                act.wait_ge(ln_recip, k + 1)
                act.activation(rstd, inv_var, ACT.Sqrt).then_inc(ln_root, 1)
                act.wait_ge(ln_shift, k + 1)
                for m in range(TT * NBLK):
                    n, a = m // TT, m % TT
                    v = (V if k == 2 else X)[:, a, n * NB:(n + 1) * NB]
                    act.activation(v, v, ACT.Identity, bias=shift[:, a:a + 1], scale=rstd[:, a:a + 1]) \
                        .then_inc(ln_scaled, 1)
                    after(m)

            act.wait_ge(ident_in, 16)
            first_block(0, 0, T_IN0)

            def in0_out(b, half, n=NB):
                act.wait_ge(main.used, 4 * b + 4)
                act.copy(H[:, 0, bass.ds(b * NB, n)], bank[2 * half][:, 0:n]).then_inc(gemm_out_a, 1)

            with act.Fori(0, IN0_FULL // 2 - 1) as i:
                for p in range(2):
                    split(2 * i + p + 1, 2 * i + p + 1)
                    in0_out(2 * i + p, p)
            split(IN0_FULL - 1, IN0_FULL - 1)
            in0_out(IN0_FULL - 2, 0)
            act.wait_ge(trig_ready, 1)
            act.activation(sinT[:], ropet[:, 0], ACT.Sin).then_inc(trig_done, 1)
            act.activation(cosT[:], ropet[:, 1], ACT.Sin).then_inc(trig_done, 1)
            split(IN0_FULL, IN0_FULL, n=W_IN - IN0_FULL * NB)
            in0_out(IN0_FULL - 1, 1)
            in0_out(IN0_FULL, 0, W_IN - IN0_FULL * NB)
            act.wait_ge(gemm_out_a, IN0_FULL + 1)
            act.wait_ge(gemm_out_v, IN0_FULL + 1)

            def filled(name, i=0):
                act.wait_ge(att_filled, FILL_AT[(name, i)] + 1)
                return bank[FILL_AT[(name, i)] % 8]

            def out_(ins):
                ins.then_inc(att_out_a, 1)

            for w in range(2):
                for a in range(TT):
                    ge(act, rms_sq, 2 * w + a - 1)
                    act.activation(la[:, a, :], H[:, a, w * RANK:(w + 1) * RANK], ACT.Square,
                                   accum_out=att[:, 2 * w + a:2 * w + a + 1]).then_inc(rms_sq, 1)
            act.wait_ge(rms_rec, 1)
            act.activation(att[:, 8:12], att[:, 4:8], ACT.Sqrt).then_inc(rms_root, 1)
            for a in range(TT):
                b = filled("gqT", a)
                out_(act.mul(gqT[:, :, a * P:(a + 1) * P], b[:].rearrange("p (h s) -> p h s", h=GH), GDK ** -0.5))
            b = filled("lrT")
            act.wait_ge(ones_set, 1)
            out_(act.copy(lrT[0:GRANK, :], b[0:GRANK, 0:SEQ]))
            b = filled("krT")
            out_(act.copy(krT[:, :], b[0:ROPE, 0:SEQ]))
            for a in range(TT):
                b = filled("z", a)
                chain(act.activation(la[:, a, :], b[:], ACT.Abs))
                chain.wait()
                chain(act.activation(la[:, a, :], la[:, a, :], ACT.Exp, scale=-1.0))
                chain.wait()
                act.activation(la[:, a, :], la[:, a, :], ACT.Ln, bias=1.0).then_inc(z_soft, 1)
            for i in range(4):
                b = filled("qn", i)
                out_(act.copy(qnT[:, 2 * i:2 * i + 2, :], b[:].rearrange("p (h s) -> p h s", h=2)))
            for a in range(TT):
                b = filled("suf", a)
                out_(act.activation(la[:, a, :], b[:], ACT.Exp))
            b = filled("dec")
            out_(act.activation(dec[:].rearrange("p h c -> p (h c)"), b[:, 0:GH * 4], ACT.Exp))
            for i in range(4):
                b = filled("kn", i)
                out_(act.copy(knT[:, 2 * i:2 * i + 2, :], b[:].rearrange("p (h s) -> p h s", h=2)))
            for i in range(4):
                b = filled("qrT", i)
                a, q = i // 2, i % 2
                out_(act.copy(qrT[:, 4 * q:4 * q + 4, a * P:(a + 1) * P],
                              b[0:ROPE, :].rearrange("p (h s) -> p h s", h=4)))
            for a in range(TT):
                v = H[:, a, GO:W_IN]
                act.activation(v, v, ACT.Silu).then_inc(go_silu, 1)
            for i in range(4):
                b = filled("ob", i)
                a, q = i // 2, i % 2
                for k in range(2):
                    m = GH * a + 2 * q + k
                    ge(act, ob_sq, m - 1)
                    act.activation(lg[:, 0, (m % 2) * GDV:(m % 2 + 1) * GDV], b[:, k * GDV:(k + 1) * GDV], ACT.Square,
                                   accum_out=att[:, 16 + m:17 + m]).then_inc(ob_sq, 1)
                if q:
                    act.wait_ge(ob_rec, a + 1)
                    act.activation(att[:, 32 + GH * a:32 + GH * (a + 1)], att[:, 24 + GH * a:24 + GH * (a + 1)],
                                   ACT.Sqrt).then_inc(ob_root, 1)
            for i in range(6):
                b = filled("s", i)
                if i < 2:
                    dst = S0[:, 4 * i:4 * i + 4, :]
                else:
                    dst = S1[:, 2 * (i - 2):2 * (i - 2) + 2, :]
                out_(act.mul(dst, b[:].rearrange("p (h s) -> p h s", h=dst.shape[1]), (NOPE + ROPE) ** -0.5))
            for a, S in enumerate((S0, S1)):
                act.wait_ge(s_shifted, a + 1)
                act.activation(S[:], S[:], ACT.Exp).then_inc(p_ready, 1)
                for i in (2 * a, 2 * a + 1):
                    b = filled("v", i)
                    half, ta = i // 2, i % 2
                    out_(act.copy(vv[:, ta, half * NB:(half + 1) * NB], b[:]))
            for i in range(6):
                b = filled("pT", i)
                if i < 2:
                    dst = pT0[:, 4 * i:4 * i + 4, :]
                else:
                    dst = pT1[:, 2 * (i - 2):2 * (i - 2) + 2, :, :].rearrange("p h k s -> p (h k) s")
                out_(act.copy(dst, b[:].rearrange("p (h s) -> p h s", h=4)))

            split(SB_OUT0, land_block(SB_OUT0), js=[0])
            first_block(SB_OUT0, land_block(SB_OUT0), T_OUT0, done=1)
            for b in range(1, NBLK):
                split(SB_OUT0 + b, land_block(SB_OUT0 + b))

            def tokens_out(s, pair, qs, used=None):
                for q in qs:
                    act.wait_ge(s.xg_fill_h, 8 * pair + q + 1)
                    if used is not None:
                        act.wait_ge(s.used, used + q // 2 + 1)
                    act.copy(xg_hi[:, 2 * q:2 * q + 2, :], bank[4 + 2 * (q % 2)][:].rearrange("p (c s) -> p c s", c=2)) \
                        .then_inc(s.xg_out_h, 1)

            def experts(s, sb0, p0, lb0):
                if s is not main:
                    split(sb0, lb0, s)
                tokens_out(s, p0, range(8))

                def body(p, first, last):
                    pair, B, L = p0 + p, sb0 + 6 * p, lb0 + 6 * p
                    E0, E1 = 2 * pair, 2 * pair + 1

                    def ahead(b, js=range(4)):
                        split(B + b, L + b, s, js=js)

                    def silu(E, b):
                        act.wait_ge(s.used, 4 * (B + b) + 4)
                        ge(act, s.h_done, E)
                        act.activation(gsil[:], bank[0][:], ACT.Silu).then_inc(s.silu_done, 1)

                    def slots(E):
                        act.wait_ge(s.pt_fill, E + 1)
                        act.copy(placeT[:], bank[2][:, 0:SEQ]).then_inc(s.pt_done, 1)

                    def hidden(E):
                        act.wait_ge(s.hT_fill, E + 1)
                        act.copy(hT_hi[:], bank[3][:].rearrange("p (c s) -> p c s", c=4)).then_inc(s.hT_hi_done, 1)

                    def y_out(E, b, n):
                        act.wait_ge(s.used, 4 * (B + b) + n + 1)
                        ge(act, s.scat_fill, 4 * E + n - 1)
                        act.copy(y_hi[:, n % 2, :], bank[2 + n % 2][:]).then_inc(s.y_hi_done, 1)

                    ahead(1)
                    silu(E0, 0)
                    ahead(2)
                    ahead(3, [0, 1])
                    slots(E0)
                    hidden(E0)
                    ahead(3, [2, 3])
                    silu(E1, 2)
                    for n in range(4):
                        y_out(E0, 3, n)
                        ahead(4, [n])
                    ahead(5, [0, 1])
                    if not last:
                        tokens_out(s, pair + 1, [0, 1], 4 * (B + 4))
                    ahead(5, [2])
                    if not last:
                        tokens_out(s, pair + 1, [2, 3], 4 * (B + 4))
                    slots(E1)
                    if not last:
                        tokens_out(s, pair + 1, [4, 5], 4 * (B + 4))
                    hidden(E1)
                    if not last:
                        tokens_out(s, pair + 1, [6, 7], 4 * (B + 4))
                    ahead(5, [3])
                    for n in range(4):
                        y_out(E1, 5, n)
                        if not last:
                            ahead(6, [n])
                over_pairs(act, body)

            def moe(layer):
                sb0 = (SB_MOE0, SB_MOE1)[layer]

                def transposed_out(g):
                    act.wait_ge(r_filled, 8 * layer + g + 1)
                    q, a = g // 2, g % 2
                    act.copy(rt[:, q % 2, :, a * P:(a + 1) * P], bank[4 + a][:].rearrange("p (c s) -> p c s", c=4)) \
                        .then_inc(r_out, 1)

                def high(k):
                    n, a = k // TT, k % TT
                    act.wait_ge(x_ready, 16 * layer + k + 1)
                    act.copy(x_hi[:, a, n * NB:(n + 1) * NB], X[:, a, n * NB:(n + 1) * NB]).then_inc(x_high, 1)

                layer_norm((0, 3)[layer], lambda m: transposed_out(m - 3) if m >= 3 else None)
                high(0)
                for g in (5, 6, 7):
                    transposed_out(g)
                    high(2 * g - 9)
                    high(2 * g - 8)
                high(7)
                act.wait_ge(logits_done, 2 * layer + 1)
                act.copy(logitsT[:, :], bank[7][0:NEXP, 0:SEQ]).then_inc(logits_out, 1)
                act.wait_ge(logits_done, 2 * layer + 2)
                act.activation(route[:, 0], bank[6][:, 0:TT * NEXP].rearrange("p (a e) -> p a e", a=TT), ACT.Sigmoid) \
                    .then_inc(sigm_done, 1)
                split(sb0, land_block(sb0))
                experts(main, sb0, layer * NPAIR, land_block(sb0))
                act.wait_ge(flag_ready, layer + 1)
                many = act.value_load(flag[0:1, layer:layer + 1])
                with act.If(many > CAP):
                    act.wait_ge(main.used, 4 * (sb0 + 3 * NEXP))
                    act.wait_ge(main.scat_fill, 4 * NEXP * (layer + 1))
                    experts(overflow[layer], 0, 0, 0)
                if layer == 0:
                    split(SB_IN1, land_block(SB_IN1), js=[0, 1])
                layer_norm((1, 4)[layer], lambda m: transposed(T_IN1, m - 3) if layer == 0 and m >= 3 else None)

            moe(0)
            lb1 = land_block(SB_IN1)
            split(SB_IN1, lb1, js=[2, 3])
            for g in (5, 6, 7):
                transposed(T_IN1, g)

            def in1_out(b, half, dst, n):
                act.wait_ge(main.used, 4 * (SB_IN1 + b) + 4)
                for a in range(TT):
                    act.activation(dst[:, a, bass.ds(n * NB, NB)], bank[2 * half + a][:], ACT.Gelu_apprx_tanh) \
                        .then_inc(gemm_out_a, 1)

            split(SB_IN1 + 1, lb1 + 1)
            in1_out(0, 0, V, 0)
            split(SB_IN1 + 2, lb1 + 2)
            in1_out(1, 1, V, 1)
            for i in range(4):
                act.wait_ge(sgu_filled, i + 1)
                act.copy(ws[:, 4 * i:4 * i + 4, :], bank[4 + i][:].rearrange("p (g s) -> p g s", g=4)) \
                    .then_inc(wsT_copied, 1)
            for b in range(2, NBLK):
                split(SB_IN1 + b + 1, lb1 + b + 1)
                in1_out(b, b % 2, V, b)
                if b == 2:
                    act.wait_ge(sgu_filled, 5)
                    act.copy(bsT[:], bank[4][:, 0:GROUPS]).then_inc(wsT_copied, 1)
            act.wait_ge(gemm_out_a, IN0_FULL + 1 + 8)
            layer_norm(2)
            for b in range(NBLK):
                split(SB_IN1 + 5 + b, lb1 + 5 + b)
                in1_out(4 + b, b % 2, U, b)
            for g in range(8):
                transposed(T_OUT1, g)
            for b in range(1, NBLK):
                split(SB_OUT1 + b, land_block(SB_OUT1 + b))
            moe(1)

        @block.vector
        def _(dve):
            chain = Chain(dve, chain_v)

            def split(sb, s=main, n=NB, js=range(4)):
                for j in js:
                    dve.wait_ge(s.hi_done, 4 * sb + j + 1)
                    dve.tensor_tensor(w_lo[:, j, 0:4 * n], w_land[:, j, 0:4 * n], w_hi[:, j, 0:4 * n], ALU.subtract) \
                        .then_inc(s.lo_done[j], 1)

            def transposed(t0, g):
                q, a = g // 2, g % 2
                dve.wait_ge(t_high, t0 + g + 1)
                v = (slice(None), slice(4 * q, 4 * q + 4), slice(a * P, (a + 1) * P))
                dve.tensor_tensor(xT_lo[v], bank[4 + (g + 2) % 4][:].rearrange("p (c s) -> p c s", c=4), xT_hi[v],
                                  ALU.subtract).then_inc(t_low, 1)

            def first_block(sb, t0, done=0):
                for j in range(2):
                    transposed(t0, 2 * j)
                    transposed(t0, 2 * j + 1)
                    if j >= done:
                        split(sb, js=[j])
                split(sb, js=[2, 3])
                for g in range(4, 8):
                    transposed(t0, g)

            def block_stats(x, a, n):
                chain(dve.bn_stats(stats[:, a, n, :], x[:, a, n * NB:(n + 1) * NB]))

            def layer_norm(k, x, signal, after=lambda m: None):
                chain.wait()
                for a in range(TT):
                    chain(dve.bn_aggr(meanvar[:, a, :], stats[:, a].rearrange("p n s -> p (n s)")))
                chain.wait()
                chain(dve.tensor_scalar(inv_var, meanvar[:, :, 1], EPS, None, ALU.add))
                chain.wait()
                dve.reciprocal(inv_var, inv_var).then_inc(ln_recip, 1)
                dve.wait_ge(ln_root, k + 1)
                dve.scalar_tensor_tensor(shift, meanvar[:, :, 0], -1.0, rstd, ALU.mult, ALU.mult) \
                    .then_inc(ln_shift, 1)
                dve.wait_ge(rows_in, 32 * (k + 1))
                columns = [slice(n * NB, (n + 1) * NB) for n in range(NBLK)]
                views = [(x[:, m % TT, columns[m // TT]], rows[:, 0, columns[m // TT]], rows[:, 1, columns[m // TT]])
                         for m in range(TT * NBLK)]
                for m in range(TT * NBLK + 1):
                    if m < TT * NBLK:
                        v, g, _ = views[m]
                        dve.wait_ge(ln_scaled, TT * NBLK * k + m + 1)
                        chain(dve.tensor_tensor(v, v, g, ALU.mult))
                    if m:
                        v, _, b = views[m - 1]
                        dve.wait_ge(chain_v, chain.n - (1 if m < TT * NBLK else 0))
                        dve.tensor_tensor(v, v, b, ALU.add).then_inc(signal, 1)
                        after(m - 1)
                dve.wait_ge(signal, {0: 8, 1: 16, 2: 8, 3: 24, 4: 32}[k])
                dve.sem_inc(rows_used, 1)

            first_block(0, T_IN0)

            def in0_out(b, half, n=NB):
                dve.wait_ge(main.used, 4 * b + 4)
                dve.tensor_copy(H[:, 1, bass.ds(b * NB, n)], bank[2 * half + 1][:, 0:n]).then_inc(gemm_out_v, 1)

            with dve.Fori(0, IN0_FULL // 2 - 1) as i:
                for p in range(2):
                    split(2 * i + p + 1)
                    in0_out(2 * i + p, p)
            dve.wait_ge(ident_in, 16)
            dve.wait_ge(const_in, 16 * 6)
            chain(dve.tensor_copy(posf[:], posi[:]))
            chain.wait()
            for a in range(TT):
                chain(dve.tensor_scalar(ropet[:, 2, a, :], cst("inv_freq"), posf[:, a:a + 1], None, ALU.mult))
            chain.wait()
            ang, sarg, carg, tmp = (ropet[:, i] for i in (2, 0, 1, 3))
            chain(dve.tensor_scalar(tmp, ang, 1.0 / (2 * np.pi), ROUND, ALU.mult, ALU.add))
            chain.wait()
            chain(dve.tensor_scalar(tmp, tmp, -ROUND, None, ALU.add))
            chain.wait()
            for i, part in enumerate((C2PI_A, C2PI_B, C2PI_C)):
                chain(dve.scalar_tensor_tensor(sarg, tmp, -part, sarg if i else ang, ALU.mult, ALU.add))
                chain.wait()

            def wrap(v):
                for limit, op, back in ((np.pi, ALU.is_gt, -2 * np.pi), (-np.pi, ALU.is_lt, 2 * np.pi)):
                    chain(dve.tensor_scalar(tmp, v, float(limit), float(back), op, ALU.mult))
                    chain.wait()
                    chain(dve.tensor_tensor(v, v, tmp, ALU.add))
                    chain.wait()

            wrap(sarg)
            chain(dve.tensor_scalar(carg, sarg, float(np.pi / 2), None, ALU.add))
            chain.wait()
            wrap(carg)
            chain(dve.tensor_scalar(sarg, sarg, PI_IN, -PI_IN, ALU.min, ALU.max))
            dve.tensor_scalar(carg, carg, PI_IN, -PI_IN, ALU.min, ALU.max).then_inc(trig_ready, 1)

            split(IN0_FULL - 1)
            in0_out(IN0_FULL - 2, 0)
            split(IN0_FULL, n=W_IN - IN0_FULL * NB)
            in0_out(IN0_FULL - 1, 1)
            in0_out(IN0_FULL, 0, W_IN - IN0_FULL * NB)
            dve.memset(lrT[:], 1.0).then_inc(ones_set, 1)
            dve.wait_ge(gemm_out_a, IN0_FULL + 1)
            dve.wait_ge(gemm_out_v, IN0_FULL + 1)

            def filled(name, i=0):
                dve.wait_ge(att_filled, FILL_AT[(name, i)] + 1)
                return bank[FILL_AT[(name, i)] % 8]

            def out_(ins):
                ins.then_inc(att_out_v, 1)

            def heads_of(x, n):
                return x.unsqueeze(1).to_broadcast([P, n, x.shape[1]])

            dve.wait_ge(trig_done, 2)
            k1, k2 = H[:, :, KR:KR + HALF], H[:, :, KR + HALF:KR + ROPE]
            chain(dve.tensor_tensor(ropet[:, 0], k1, cosT[:], ALU.mult))
            chain(dve.tensor_tensor(ropet[:, 1], k2, sinT[:], ALU.mult))
            chain(dve.tensor_tensor(ropet[:, 2], k2, cosT[:], ALU.mult))
            chain(dve.tensor_tensor(ropet[:, 3], k1, sinT[:], ALU.mult))
            chain.wait()
            chain(dve.tensor_tensor(kr_rot[:, :, 0:HALF], ropet[:, 0], ropet[:, 1], ALU.subtract))
            dve.tensor_tensor(kr_rot[:, :, HALF:ROPE], ropet[:, 2], ropet[:, 3], ALU.add).then_inc(kr_rotated, 1)
            dve.wait_ge(rms_sq, 4)
            chain(dve.tensor_scalar(att[:, 4:8], att[:, 0:4], 1.0 / RANK, EPS, ALU.mult, ALU.add))
            chain.wait()
            dve.reciprocal(att[:, 4:8], att[:, 4:8]).then_inc(rms_rec, 1)
            dve.wait_ge(rms_root, 1)
            for w in range(2):
                for a in range(TT):
                    v = H[:, a, w * RANK:(w + 1) * RANK]
                    dve.tensor_scalar(v, v, att[:, 8 + 2 * w + a:9 + 2 * w + a], None, ALU.mult) \
                        .then_inc(c_normed, 1)
            for w, (name, dst) in enumerate((("cqT", cqT), ("ckvT", ckvT))):
                for a in range(TT):
                    b = filled(name, a)
                    out_(dve.tensor_tensor(dst[:, :, a * P:(a + 1) * P], b[:].rearrange("p (c s) -> p c s", c=4),
                                           gains[:, w, :].unsqueeze(2).to_broadcast([P, 4, P]), ALU.mult))
            for a in range(TT):
                b = filled("z", a)
                dve.wait_ge(z_soft, a + 1)
                out_(dve.scalar_tensor_tensor(lg[:, a, :], b[:], 0.0, la[:, a, :], ALU.min, ALU.subtract))
                dve.wait_ge(att_out_v, EMPTIED[("z", a)][1])
                dve.sem_inc(logg_ready, 1)
            for a in range(TT):
                b = filled("qr", a)[:].rearrange("p (h d) -> p h d", h=HEADS)
                q1, q2 = b[:, :, 0:HALF], b[:, :, HALF:ROPE]
                cos, sin = heads_of(cosT[:, a, :], HEADS), heads_of(sinT[:, a, :], HEADS)
                chain(dve.tensor_tensor(rtmp[:, 0], q1, cos, ALU.mult))
                chain(dve.tensor_tensor(rtmp[:, 1], q2, sin, ALU.mult))
                chain.wait()
                chain(dve.tensor_tensor(qrr[:, a, :, 0:HALF], rtmp[:, 0], rtmp[:, 1], ALU.subtract))
                chain.wait()
                chain(dve.tensor_tensor(rtmp[:, 0], q2, cos, ALU.mult))
                out_(dve.tensor_tensor(rtmp[:, 1], q1, sin, ALU.mult))
                chain.wait()
                dve.wait_ge(att_out_v, EMPTIED[("qr", a)][1])
                dve.tensor_tensor(qrr[:, a, :, HALF:ROPE], rtmp[:, 0], rtmp[:, 1], ALU.add).then_inc(qr_rotated, 1)
                dve.wait_ge(qr_rotated, a + 1)
            for a in range(TT):
                dve.wait_ge(att_out_a, EMPTIED[("suf", a)][1])
                dve.tensor_tensor(kdec[:, a, :], H[:, a, GK:GK + GH * GDK], la[:, a, :], ALU.mult) \
                    .then_inc(kdec_ready, 1)
            dve.wait_ge(att_out_a, EMPTIED[("dec", 0)][1])
            for i in range(8):
                b = filled("upd", i)
                for k in range(2):
                    c, h = (2 * i + k) // GH, (2 * i + k) % GH
                    upd = b[:, k * GDV:(k + 1) * GDV]
                    if c == 0:
                        ins = dve.tensor_copy(states[:, h, 0, :], upd)
                    else:
                        dve.wait_ge(att_out_v, EMPTIED[("upd", i - 2)][1])
                        dve.wait_ge(chain_v, chain.n)
                        ins = dve.scalar_tensor_tensor(states[:, h, c, :], states[:, h, c - 1, :],
                                                       dec[:, h, c:c + 1], upd, ALU.mult, ALU.add)
                    (out_ if k else chain)(ins)
            for a in range(TT):
                dve.wait_ge(go_silu, a + 1)
                v = H[:, a, GO:W_IN].rearrange("p (h d) -> p h d", h=GH)
                chain(dve.tensor_tensor(v, v, heads_of(gnorm[:], GH), ALU.mult))
            for a in range(TT):
                dve.wait_ge(ob_sq, GH * (a + 1))
                m = att[:, 24 + GH * a:24 + GH * (a + 1)]
                chain(dve.tensor_scalar(m, att[:, 16 + GH * a:16 + GH * (a + 1)], 1.0 / GDV, EPS, ALU.mult, ALU.add))
                chain.wait()
                dve.reciprocal(m, m).then_inc(ob_rec, 1)
                dve.wait_ge(ob_root, a + 1)
                for q in range(2):
                    b = filled("ob", 2 * a + q)
                    for k in range(2):
                        h = 2 * q + k
                        ins = dve.scalar_tensor_tensor(
                            H[:, a, GV + h * GDV:GV + (h + 1) * GDV], b[:, k * GDV:(k + 1) * GDV],
                            att[:, 32 + GH * a + h:33 + GH * a + h], H[:, a, GO + h * GDV:GO + (h + 1) * GDV],
                            ALU.mult, ALU.mult)
                        (out_ if k else chain)(ins)
            for a, S in enumerate((S0, S1)):
                keys = P * (a + 1)
                dve.wait_ge(att_out_a, EMPTIED[("s", (1, 5)[a])][1])
                chain(dve.memset(S[0:CHUNK, :, keys - CHUNK:keys], -BIG))
                chain.wait()
                mx = att[:, 40 + HEADS * a:40 + HEADS * (a + 1)]
                chain(dve.tensor_reduce(mx, S[:], AX_X, ALU.max))
                chain.wait()
                dve.tensor_tensor(S[:], S[:], mx.unsqueeze(2).to_broadcast([P, HEADS, keys]), ALU.subtract) \
                    .then_inc(s_shifted, 1)
            for a, S in enumerate((S0, S1)):
                dve.wait_ge(p_ready, a + 1)
                chain(dve.tensor_reduce(att[:, 56 + HEADS * a:56 + HEADS * (a + 1)], S[:], AX_X, ALU.add))
            chain.wait()
            chain(dve.reciprocal(att[:, 72:88], att[:, 56:72]))
            chain.wait()
            for i in range(4):
                a, q = i // 2, i % 2
                if i == 1:
                    split(SB_OUT0, js=[0])
                b = filled("o", i)
                r = att[:, 72 + HEADS * a + 4 * q:72 + HEADS * a + 4 * q + 4]
                out_(dve.tensor_tensor(H[:, a, q * NB:(q + 1) * NB].rearrange("p (h d) -> p h d", h=4),
                                       b[:].rearrange("p (h d) -> p h d", h=4),
                                       r.unsqueeze(2).to_broadcast([P, 4, VD]), ALU.mult))

            def out_projection(sb0, ev0):
                for b in range(NBLK):
                    if b + 1 < NBLK:
                        split(sb0 + b + 1)
                    dve.wait_ge(main.used, 4 * (sb0 + b) + 4)
                    for a in range(TT):
                        v = X[:, a, b * NB:(b + 1) * NB]
                        dve.scalar_tensor_tensor(v, v, ALPHA, bank[2 * (b % 2) + a][:], ALU.mult, ALU.add) \
                            .then_inc(gemm_out_v, 1)
                    for a in range(TT):
                        dve.wait_ge(gemm_out_v, ev0 + 2 * b + a + 1)
                        block_stats(X, a, b)

            first_block(SB_OUT0, T_OUT0, done=1)
            out_projection(SB_OUT0, IN0_FULL + 1)

            def route_tokens(layer):
                r = [route[:, i] for i in range(16)]
                score, biased, ing, e1, oh1, masked, sel = r[0], r[1], r[2], r[3], r[4], r[5], r[15]
                q = [r[7][:, :, 4 * i:4 * i + 4] for i in range(4)] + [r[8][:, :, 4 * i:4 * i + 4] for i in range(4)]
                one = [r[9][:, :, i:i + 1] for i in range(8)]
                dve.wait_ge(sigm_done, layer + 1)

                def step(ins):
                    chain(ins)
                    chain.wait()

                def tt(out_ap, x, y, op):
                    step(dve.tensor_tensor(out_ap, x, y, op))

                step(dve.tensor_tensor(biased, score, rbias[:].unsqueeze(1).to_broadcast([P, TT, NEXP]), ALU.add))
                g = biased.rearrange("p a (g e) -> p a g e", g=NGRP)
                a0, a1, a2, a3 = (g[:, :, :, i] for i in range(EPG))
                hi1, lo1, hi2, lo2, top, m1, m2, gs = q
                tt(hi1, a0, a1, ALU.max)
                tt(lo1, a0, a1, ALU.min)
                tt(hi2, a2, a3, ALU.max)
                tt(lo2, a2, a3, ALU.min)
                tt(top, hi1, hi2, ALU.max)
                tt(m1, hi1, hi2, ALU.min)
                tt(m2, lo1, lo2, ALU.max)
                tt(m1, m1, m2, ALU.max)
                tt(gs, top, m1, ALU.add)

                def first_of(x, n, weights, best, onehot, work):
                    step(dve.tensor_reduce(best, x, AX_X, ALU.max))
                    tt(work, x, best.to_broadcast([P, TT, n]), ALU.is_equal)
                    tt(work, work, weights.unsqueeze(1).to_broadcast([P, TT, n]), ALU.mult)
                    step(dve.tensor_reduce(best, work, AX_X, ALU.max))
                    tt(onehot, work, best.to_broadcast([P, TT, n]), ALU.is_equal)

                first_of(gs, NGRP, cst("four"), one[0], hi1, lo1)
                step(dve.tensor_copy(ing.rearrange("p a (g e) -> p a g e", g=NGRP),
                                     hi1.unsqueeze(3).to_broadcast([P, TT, NGRP, EPG])))
                tt(masked, biased, ing, ALU.mult)
                step(dve.tensor_scalar(e1, ing, BIG, -BIG, ALU.mult, ALU.add))
                tt(masked, masked, e1, ALU.add)
                first_of(masked, NEXP, cst("sixteen"), one[1], oh1, e1)
                step(dve.tensor_scalar(e1, oh1, -BIG, None, ALU.mult))
                step(dve.tensor_scalar(r[6], oh1, -1.0, 1.0, ALU.mult, ALU.add))
                tt(masked, masked, r[6], ALU.mult)
                tt(masked, masked, e1, ALU.add)
                first_of(masked, NEXP, cst("sixteen"), one[2], r[10], r[11])
                chain(dve.tensor_tensor(sel, oh1, r[10], ALU.add))
                chain.wait()
                dve.sem_inc(sel_ready, 1)
                tt(r[12], score, sel, ALU.mult)
                step(dve.tensor_reduce(one[3], r[12], AX_X, ALU.add))
                step(dve.reciprocal(one[4], one[3]))
                tt(comb[:], r[12], one[4].to_broadcast([P, TT, NEXP]), ALU.mult)
                step(dve.tensor_scalar(r[13], sel, -FAR, FAR, ALU.mult, ALU.add))
                dve.wait_ge(rank_done, layer + 1)
                got = bank[6][:, 64:128].rearrange("p (a e) -> p a e", a=TT)[:, :, 0:NEXP]
                dve.tensor_tensor(rank[:], got, r[13], ALU.add).then_inc(rank_ready, 1)
                dve.wait_ge(rank_ready, layer + 1)
                for k in range(2):
                    for a in range(TT):
                        ins = dve.tensor_scalar(place_r[:, a, k * CAP:(k + 1) * CAP], cst("iota0"),
                                                rank[:, a, k:k + 1], None, ALU.is_equal)
                ins.then_inc(main.place_r_ready, 1)
                step(dve.tensor_reduce(flagf[:, layer:layer + 1], bank[6][:, 128:128 + NEXP], AX_X, ALU.max))
                dve.tensor_copy(flag[:, layer:layer + 1], flagf[:, layer:layer + 1]).then_inc(flag_ready, 1)

            def tokens_out(s, pair, qs, used=None):
                for q in qs:
                    dve.wait_ge(s.xg_fill_l, 8 * pair + q + 1)
                    if used is not None:
                        dve.wait_ge(s.used, used + q // 2 + 1)
                    dve.tensor_copy(xg_lo[:, 2 * q:2 * q + 2, :], bank[5 + 2 * (q % 2)][:].rearrange("p (c s) -> p c s", c=2)) \
                        .then_inc(s.xg_out_l, 1)

            def experts(s, sb0, p0):
                if s is not main:
                    split(sb0, s)
                tokens_out(s, p0, range(8))

                def add(E, n):
                    m = 4 * E + n
                    dve.wait_ge(s.scat_fill, m + 1)
                    ge(dve, s.acc_done, m - 3)
                    for a in range(TT):
                        v = X[:, a, n * NB:(n + 1) * NB]
                        ins = dve.scalar_tensor_tensor(v, bank[6 + a][:], cur[:, 3, a:a + 1], v, ALU.mult, ALU.add)
                        if a == 0:
                            ins.then_inc(s.acc0_done, 1)
                    ins.then_inc(s.acc_done, 1)

                def body(p, first, last):
                    pair, B = p0 + p, sb0 + 6 * p
                    E0, E1 = 2 * pair, 2 * pair + 1

                    def ahead(b, js=range(4)):
                        split(B + b, s, js=js)

                    def weights(e, E):
                        ge(dve, s.acc_done, 4 * E)
                        dve.tensor_copy(cur[:, 3, :], comb[:, :, bass.ds(e, 1)].rearrange("p a o -> p (a o)")) \
                            .then_inc(s.cur_v, 1)

                    def product(E, b):
                        dve.wait_ge(s.used, 4 * (B + b) + 4)
                        dve.wait_ge(s.silu_done, E + 1)
                        dve.tensor_tensor(hid[:], gsil[:], bank[1][:], ALU.mult).then_inc(s.h_done, 1)

                    def hidden(E):
                        dve.wait_ge(s.hT_hi_done, E + 1)
                        dve.tensor_tensor(hT_lo[:], bank[3][:].rearrange("p (c s) -> p c s", c=4), hT_hi[:],
                                          ALU.subtract).then_inc(s.hT_lo_done, 1)

                    def statistics(E, n):
                        dve.wait_ge(s.acc0_done, 4 * E + n + 1)
                        dve.wait_ge(s.acc_done, 4 * E + n + 1)
                        for a in range(TT):
                            block_stats(X, a, n)

                    def y_out(E, n):
                        dve.wait_ge(s.y_hi_done, 4 * E + n + 1)
                        dve.tensor_tensor(y_lo[:, n % 2, :], bank[2 + n % 2][:], y_hi[:, n % 2, :], ALU.subtract) \
                            .then_inc(s.y_lo_done, 1)
                        if n:
                            add(E, n - 1)

                    if not first:
                        add(E0 - 1, 3)
                    weights(2 * p, E0)
                    ahead(1)
                    ahead(2, range(3))
                    product(E0, 1)
                    ahead(2, [3])
                    ahead(3, [0, 1])
                    hidden(E0)
                    ahead(3, [2, 3])
                    dve.wait_ge(s.cur_v, E0 + 1)
                    if first and s is main:
                        dve.wait_ge(x_scaled, pair // NPAIR + 1)
                    for n in range(4):
                        y_out(E0, n)
                        if n not in POOL_SLOTS:
                            ahead(4, [n])
                    add(E0, 3)
                    weights(2 * p + 1, E1)
                    ahead(5, [0, 1])
                    if not last:
                        tokens_out(s, pair + 1, [0, 1], 4 * (B + 4))
                    if last:
                        product(E1, 4)
                        ahead(5, [2])
                    else:
                        ahead(5, [2])
                        tokens_out(s, pair + 1, [2, 3], 4 * (B + 4))
                        product(E1, 4)
                    if not last:
                        tokens_out(s, pair + 1, [4, 5], 4 * (B + 4))
                    hidden(E1)
                    if not last:
                        tokens_out(s, pair + 1, [6, 7], 4 * (B + 4))
                    ahead(5, [3])
                    dve.wait_ge(s.cur_v, E1 + 1)
                    for n in range(4):
                        y_out(E1, n)
                        if not last and n not in POOL_SLOTS:
                            ahead(6, [n])
                        if last and s is main and n:
                            statistics(E1, n - 1)
                    if last:
                        add(E1, 3)
                        if s is main:
                            statistics(E1, 3)
                over_pairs(dve, body)

            def moe(layer):
                layer_norm((0, 3)[layer], X, x_ready)
                for k in range(TT * NBLK):
                    n, a = k // TT, k % TT
                    v = slice(n * NB, (n + 1) * NB)
                    dve.wait_ge(x_high, 8 * layer + k + 1)
                    dve.tensor_tensor(x_lo[:, a, v], X[:, a, v], x_hi[:, a, v], ALU.subtract).then_inc(x_low, 1)
                route_tokens(layer)
                experts(main, (SB_MOE0, SB_MOE1)[layer], layer * NPAIR)
                dve.wait_ge(flag_ready, layer + 1)
                many = dve.value_load(flag[0:1, layer:layer + 1])
                with dve.If(many > CAP):
                    dve.wait_ge(main.acc_done, 4 * NEXP * (layer + 1))
                    experts(overflow[layer], 0, 0)
                    dve.wait_ge(overflow[layer].acc_done, 4 * NEXP)
                    dve.wait_ge(overflow[layer].acc0_done, 4 * NEXP)
                    for n in range(NBLK):
                        for a in range(TT):
                            dve.bn_stats(stats[:, a, n, :], X[:, a, n * NB:(n + 1) * NB]) \
                                .then_inc(overflow[layer].stats_done, 1)
                    dve.wait_ge(overflow[layer].stats_done, TT * NBLK)
                dve.wait_ge(main.acc_done, 4 * NEXP * (layer + 1))
                dve.wait_ge(main.acc0_done, 4 * NEXP * (layer + 1))
                dve.sem_inc(moe_over, 1)
                layer_norm((1, 4)[layer], X, x_ready, lambda m: transposed(T_IN1, m - 3) if layer == 0 and m >= 3
                           else None)

            moe(0)
            for g in (5, 6, 7):
                transposed(T_IN1, g)
            split(SB_IN1 + 1)
            for n in range(NBLK):
                if n < 3:
                    split(SB_IN1 + 2 + n)
                for a in range(TT):
                    dve.wait_ge(gemm_out_a, IN0_FULL + 1 + 2 * n + a + 1)
                    block_stats(V, a, n)
            layer_norm(2, V, v_ready)
            dve.wait_ge(wsT_copied, 5)
            dve.memset(ws[CHUNK:P, :, 0:CHUNK], 0.0).then_inc(wsT_ready, 1)
            split(SB_IN1 + 5)
            split(SB_IN1 + 6)

            def gate(n):
                dve.wait_ge(gemm_out_a, IN0_FULL + 1 + 8 + 2 * n + 2)
                for i in (2 * n, 2 * n + 1):
                    dve.wait_ge(sgu_filled, 5 + i + 1)
                    for k in range(2):
                        g = 2 * i + k
                        u = U[:, :, g * P:(g + 1) * P]
                        ins = dve.scalar_tensor_tensor(
                            u, bank[4 + i % 2][:, k * 2 * P:(k + 1) * 2 * P].rearrange("p (a c) -> p a c", a=TT),
                            bsT[:, g:g + 1], u, ALU.add, ALU.mult)
                        if k == 0:
                            chain(ins)
                    ins.then_inc(sgu_out, 1)

            gate(0)
            split(SB_IN1 + 7)
            gate(1)
            split(SB_OUT1)
            gate(2)
            gate(3)
            for g in range(8):
                transposed(T_OUT1, g)
            out_projection(SB_OUT1, IN0_FULL + 1 + 8)
            moe(1)


_INS = ["x", "positions", "ev_w_in", "ev_q_norm", "ev_kv_norm", "ev_w_uq", "ev_w_ukv", "ev_w_gk2", "ev_b_gk2",
        "ev_gla_norm", "ev_w_out", "od_w_in", "od_sgu_ln_g", "od_sgu_ln_b", "od_w_s", "od_b_s", "od_w_out",
        "ln_mix_g", "ln_mix_b", "ln_ffn_g", "ln_ffn_b", "router_w", "router_b", "moe_w_gate", "moe_w_up", "moe_w_down"]


def kernel(**inputs):
    import concourse.bacc as bacc
    from concourse.bass_utils import run_bass_kernel_spmd

    nc = bacc.Bacc("TRN2", target_bir_lowering=False, num_devices=1)
    arrays, A = {}, {}
    for name in _INS + ["const"]:
        a = np.ascontiguousarray(constants() if name == "const" else inputs[name])
        arrays[f"in_{name}"] = a
        A[name] = nc.dram_tensor(f"in_{name}", a.shape, mybir.dt.from_np(a.dtype), kind="ExternalInput").ap()
    out = nc.dram_tensor("out_x", (1, SEQ, D), F32, kind="ExternalOutput").ap()
    build(nc, A, out)
    r = run_bass_kernel_spmd(nc, [arrays], core_ids=[0])
    return r.results[0]["out_x"]
```
